# Optimizing a Trainium2 kernel written in Bass

```python
import jax, jax.numpy as jnp
from jax import lax
import numpy as np

D_MODEL = 1024
BATCH = 1
SEQ = 256
DEPTH = 1

HEAD_DIM = 64
N_NSA_HEADS = 8
N_NSA_KV = 2
NSA_REP = N_NSA_HEADS // N_NSA_KV
N_FOX_HEADS = 4
N_SB_HEADS = 4
D_NSA = N_NSA_HEADS * HEAD_DIM
D_FOX = N_FOX_HEADS * HEAD_DIM
D_SB = N_SB_HEADS * HEAD_DIM
D_MIX = D_NSA + D_FOX + D_SB
N_NSA_BRANCH = 3
CMP_LEN = 32
CMP_STRIDE = 16
CMP_HIDDEN = 128
SEL_LEN = 64
SEL_TOPK = 16
WINDOW = 512
Q_BLOCK = 128
N_EXPERTS = 32
TOP_K = 4
D_EXPERT = D_MODEL
SWIGLU_LIMIT = 7.0
SWIGLU_ALPHA = 1.702
MOE_BLOCK = 256
DEEPNORM_ALPHA = (2 * DEPTH) ** 0.25
DEEPNORM_BETA = (8 * DEPTH) ** -0.25
LN_EPS = 1e-5
RMS_EPS = 1e-6
NEG_INF = -1e30
FORGET_BIAS_INIT = 3.0

COL_NSA_Q = D_NSA
COL_NSA_KV = N_NSA_BRANCH * 2 * N_NSA_KV * HEAD_DIM
COL_NSA_GATE = N_NSA_BRANCH * N_NSA_HEADS
COL_FOX_QKV = 3 * D_FOX
COL_FOX_F = N_FOX_HEADS
COL_SB_QKV = 3 * D_SB
OFF_NSA_KV = COL_NSA_Q
OFF_NSA_GATE = OFF_NSA_KV + COL_NSA_KV
OFF_FOX_QKV = OFF_NSA_GATE + COL_NSA_GATE
OFF_FOX_F = OFF_FOX_QKV + COL_FOX_QKV
OFF_SB_QKV = OFF_FOX_F + COL_FOX_F
D_IN = OFF_SB_QKV + COL_SB_QKV

kernel_name = "hybrid_nsa_fox_stickbreak_moe_deepnorm"

F32 = jnp.float32

def layer_norm(x, g, b):
    xf = x.astype(F32)
    mu = jnp.mean(xf, axis=-1, keepdims=True)
    var = jnp.mean(jnp.square(xf - mu), axis=-1, keepdims=True)
    return ((xf - mu) * lax.rsqrt(var + LN_EPS) * g + b).astype(x.dtype)

def rms_norm(x, g):
    xf = x.astype(F32)
    return xf * lax.rsqrt(jnp.mean(jnp.square(xf), axis=-1, keepdims=True) + RMS_EPS) * g

def masked_softmax(s, mask):
    s = jnp.where(mask, s.astype(F32), NEG_INF)
    p = jax.nn.softmax(s, axis=-1)
    return p * jnp.any(mask, axis=-1, keepdims=True)

def alibi_slopes(n):
    return jnp.exp2(-8.0 * jnp.arange(1, n + 1, dtype=F32) / n)

def blocks_to_seq(o):
    nqb, b, h, qb, d = o.shape
    return o.transpose(1, 0, 3, 2, 4).reshape(b, nqb * qb, h * d)

def nsa_attention(q, k_br, v_br, gates, pos_k, pos_v, w1_k, w2_k, w1_v, w2_v):
    B, H, S, dh = q.shape
    G, R = N_NSA_KV, NSA_REP
    scale = dh ** -0.5
    kc, ks, kw = k_br[0], k_br[1], k_br[2]
    vc, vs, vw = v_br[0], v_br[1], v_br[2]
    n_cmp = (S - CMP_LEN) // CMP_STRIDE + 1
    cmp_idx = jnp.arange(n_cmp)[:, None] * CMP_STRIDE + jnp.arange(CMP_LEN)[None, :]
    cmp_end = cmp_idx[:, -1]

    def compress(kv, pos, w1, w2):
        blk = kv[:, :, cmp_idx] + pos
        hid = jax.nn.gelu(blk.reshape(B, G, n_cmp, CMP_LEN * dh) @ w1)
        return hid @ w2

    k_cmp = compress(kc, pos_k, w1_k, w2_k)
    v_cmp = compress(vc, pos_v, w1_v, w2_v)
    n_blk = S // SEL_LEN
    n_sel = min(SEL_TOPK, n_blk)
    overlap = jax.nn.one_hot(cmp_idx // SEL_LEN, n_blk, dtype=F32).mean(axis=1)
    ks_blk = ks.reshape(B, G, n_blk, SEL_LEN, dh)
    vs_blk = vs.reshape(B, G, n_blk, SEL_LEN, dh)
    kw_pad = jnp.pad(kw, ((0, 0), (0, 0), (WINDOW, 0), (0, 0)))
    vw_pad = jnp.pad(vw, ((0, 0), (0, 0), (WINDOW, 0), (0, 0)))
    slopes = alibi_slopes(H).reshape(1, G, R, 1, 1)
    b_ix = jnp.arange(B)[:, None, None, None]
    g_ix = jnp.arange(G)[None, :, None, None]
    blk_ids = jnp.arange(n_blk)
    sel_off = jnp.arange(SEL_LEN)
    win_off = jnp.arange(Q_BLOCK + WINDOW)

    def block(i):
        q0 = i * Q_BLOCK
        t = q0 + jnp.arange(Q_BLOCK)
        tf = t.astype(F32)
        qb = lax.dynamic_slice_in_dim(q, q0, Q_BLOCK, axis=2).reshape(B, G, R, Q_BLOCK, dh)
        gb = lax.dynamic_slice_in_dim(gates, q0, Q_BLOCK, axis=2).reshape(B, G, R, Q_BLOCK, N_NSA_BRANCH)
        s_c = jnp.einsum('bgrqd,bgnd->bgrqn', qb, k_cmp).astype(F32) * scale \
            - slopes * (tf[:, None] - cmp_end[None, :].astype(F32))
        p_c = masked_softmax(s_c, cmp_end[None, :] <= t[:, None])
        o_c = jnp.einsum('bgrqn,bgnd->bgrqd', p_c, v_cmp)
        imp = jnp.einsum('bgrqn,nj->bgqj', p_c, overlap)
        cur = (t // SEL_LEN)[:, None]
        valid = blk_ids[None, :] <= cur
        forced = valid & ((blk_ids[None, :] == 0) | (blk_ids[None, :] >= cur - 1))
        imp = jnp.where(forced, jnp.inf, jnp.where(valid, imp, -jnp.inf))
        _, sel = lax.top_k(imp, n_sel)
        k_sel = ks_blk[b_ix, g_ix, sel].reshape(B, G, Q_BLOCK, n_sel * SEL_LEN, dh)
        v_sel = vs_blk[b_ix, g_ix, sel].reshape(B, G, Q_BLOCK, n_sel * SEL_LEN, dh)
        pos_sel = (sel[..., None] * SEL_LEN + sel_off).reshape(B, G, Q_BLOCK, n_sel * SEL_LEN)
        dist_sel = t[None, None, :, None] - pos_sel
        s_s = jnp.einsum('bgrqd,bgqkd->bgrqk', qb, k_sel).astype(F32) * scale \
            - slopes * dist_sel[:, :, None].astype(F32)
        p_s = masked_softmax(s_s, (dist_sel >= 0)[:, :, None])
        o_s = jnp.einsum('bgrqk,bgqkd->bgrqd', p_s, v_sel)
        k_win = lax.dynamic_slice_in_dim(kw_pad, q0, Q_BLOCK + WINDOW, axis=2)
        v_win = lax.dynamic_slice_in_dim(vw_pad, q0, Q_BLOCK + WINDOW, axis=2)
        pos_w = q0 - WINDOW + win_off
        dist_w = t[:, None] - pos_w[None, :]
        mask_w = (pos_w[None, :] >= 0) & (dist_w >= 0) & (dist_w < WINDOW)
        s_w = jnp.einsum('bgrqd,bgkd->bgrqk', qb, k_win).astype(F32) * scale \
            - slopes * dist_w.astype(F32)
        p_w = masked_softmax(s_w, mask_w)
        o_w = jnp.einsum('bgrqk,bgkd->bgrqd', p_w, v_win)
        o = gb[..., 0:1] * o_c + gb[..., 1:2] * o_s + gb[..., 2:3] * o_w
        return o.reshape(B, H, Q_BLOCK, dh)

    return blocks_to_seq(lax.map(block, jnp.arange(S // Q_BLOCK)))

def forgetting_attention(q, k, v, log_f):
    B, H, S, dh = q.shape
    scale = dh ** -0.5
    c = jnp.cumsum(log_f, axis=-1)
    key_pos = jnp.arange(S)

    def block(i):
        q0 = i * Q_BLOCK
        t = q0 + jnp.arange(Q_BLOCK)
        qb = lax.dynamic_slice_in_dim(q, q0, Q_BLOCK, axis=2)
        cb = lax.dynamic_slice_in_dim(c, q0, Q_BLOCK, axis=2)
        s = jnp.einsum('bhqd,bhkd->bhqk', qb, k).astype(F32) * scale \
            + cb[..., :, None] - c[..., None, :]
        p = masked_softmax(s, key_pos[None, :] <= t[:, None])
        return jnp.einsum('bhqk,bhkd->bhqd', p, v)

    return blocks_to_seq(lax.map(block, jnp.arange(S // Q_BLOCK)))

def stick_breaking_attention(q, k, v):
    B, H, S, dh = q.shape
    scale = dh ** -0.5
    key_pos = jnp.arange(S)

    def block(i):
        q0 = i * Q_BLOCK
        t = q0 + jnp.arange(Q_BLOCK)
        qb = lax.dynamic_slice_in_dim(q, q0, Q_BLOCK, axis=2)
        z = jnp.einsum('bhqd,bhkd->bhqk', qb, k).astype(F32) * scale
        strict = key_pos[None, :] < t[:, None]
        log_beta = jax.nn.log_sigmoid(z)
        log_keep = jnp.where(strict, jax.nn.log_sigmoid(-z), 0.0)
        shifted = jnp.concatenate([log_keep[..., 1:], jnp.zeros_like(log_keep[..., :1])], axis=-1)
        later = lax.cumsum(shifted, axis=3, reverse=True)
        a = jnp.where(strict, jnp.exp(log_beta + later), 0.0)
        return jnp.einsum('bhqk,bhkd->bhqd', a, v)

    return blocks_to_seq(lax.map(block, jnp.arange(S // Q_BLOCK)))

def hybrid_mixer(x, w_in, b_in, pos_k, pos_v, w1_k, w2_k, w1_v, w2_v, g_out, w_out):
    B, S, _ = x.shape
    proj = x @ w_in + b_in
    q_nsa = proj[..., :OFF_NSA_KV].reshape(B, S, N_NSA_HEADS, HEAD_DIM).transpose(0, 2, 1, 3)
    kv_nsa = proj[..., OFF_NSA_KV:OFF_NSA_GATE].reshape(
        B, S, N_NSA_BRANCH, 2, N_NSA_KV, HEAD_DIM).transpose(2, 3, 0, 4, 1, 5)
    gates = jax.nn.sigmoid(proj[..., OFF_NSA_GATE:OFF_FOX_QKV].reshape(
        B, S, N_NSA_BRANCH, N_NSA_HEADS)).transpose(0, 3, 1, 2)
    fox = proj[..., OFF_FOX_QKV:OFF_FOX_F].reshape(B, S, 3, N_FOX_HEADS, HEAD_DIM).transpose(2, 0, 3, 1, 4)
    log_f = jax.nn.log_sigmoid(proj[..., OFF_FOX_F:OFF_SB_QKV].astype(F32)).transpose(0, 2, 1)
    sb = proj[..., OFF_SB_QKV:].reshape(B, S, 3, N_SB_HEADS, HEAD_DIM).transpose(2, 0, 3, 1, 4)
    o_nsa = nsa_attention(q_nsa, kv_nsa[:, 0], kv_nsa[:, 1], gates, pos_k, pos_v, w1_k, w2_k, w1_v, w2_v)
    o_fox = forgetting_attention(fox[0], fox[1], fox[2], log_f)
    o_sb = stick_breaking_attention(sb[0], sb[1], sb[2])
    o = jnp.concatenate([
        rms_norm(o_nsa, g_out[:D_NSA]),
        rms_norm(o_fox, g_out[D_NSA:D_NSA + D_FOX]),
        rms_norm(o_sb, g_out[D_NSA + D_FOX:]),
    ], axis=-1).astype(x.dtype)
    return o @ w_out

def moe_ffn(h, router_w, router_b, w_gu, b_gu, w_dn, b_dn):
    B, S, D = h.shape
    T = B * S
    M = T * TOP_K
    xt = h.reshape(T, D)
    logits = (xt @ router_w + router_b).astype(F32)
    top_logit, top_e = lax.top_k(logits, TOP_K)
    top_w = jax.nn.softmax(top_logit, axis=-1)
    flat_e = top_e.reshape(M)
    flat_tok = jnp.repeat(jnp.arange(T, dtype=jnp.int32), TOP_K)
    flat_w = top_w.reshape(M)
    order = jnp.argsort(flat_e)
    sorted_e = flat_e[order]
    counts = jnp.bincount(flat_e, length=N_EXPERTS)
    start = jnp.cumsum(counts) - counts
    padded = (counts + MOE_BLOCK - 1) // MOE_BLOCK * MOE_BLOCK
    pad_end = jnp.cumsum(padded)
    pad_start = pad_end - padded
    dest = pad_start[sorted_e] + jnp.arange(M) - start[sorted_e]
    n_blocks = -(-M // MOE_BLOCK) + N_EXPERTS
    P = n_blocks * MOE_BLOCK
    buf_tok = jnp.zeros((P,), jnp.int32).at[dest].set(flat_tok[order])
    buf_w = jnp.zeros((P,), F32).at[dest].set(flat_w[order])
    blk_e = jnp.minimum(jnp.searchsorted(pad_end, jnp.arange(n_blocks) * MOE_BLOCK, side='right'),
                        N_EXPERTS - 1)

    def expert_block(args):
        e, tok, w = args
        xb = xt[tok]
        gu = xb @ w_gu[e] + b_gu[e]
        gate = jnp.minimum(gu[:, :D_EXPERT], SWIGLU_LIMIT)
        up = jnp.clip(gu[:, D_EXPERT:], -SWIGLU_LIMIT, SWIGLU_LIMIT)
        act = gate * jax.nn.sigmoid(SWIGLU_ALPHA * gate) * (up + 1.0)
        y = act @ w_dn[e] + b_dn[e]
        return (y * w[:, None]).astype(h.dtype)

    ys = lax.map(expert_block, (blk_e, buf_tok.reshape(n_blocks, MOE_BLOCK), buf_w.reshape(n_blocks, MOE_BLOCK)))
    out = jnp.zeros((T, D), h.dtype).at[buf_tok].add(ys.reshape(P, D))
    return out.reshape(B, S, D)

def setup_inputs(seed: int = 0) -> dict:
    key = jax.random.key(seed)
    ks = jax.random.split(key, 24)
    L = DEPTH

    def nrm(k, shape, scale):
        return jax.random.normal(k, shape, F32) * scale

    x = nrm(ks[0], (BATCH, SEQ, D_MODEL), 1.0)
    w_in = nrm(ks[1], (L, D_MODEL, D_IN), D_MODEL ** -0.5)
    b_in = nrm(ks[2], (L, D_IN), 0.01).at[:, OFF_FOX_F:OFF_SB_QKV].add(FORGET_BIAS_INIT)
    cmp_pos_k = nrm(ks[3], (L, CMP_LEN, HEAD_DIM), 0.1)
    cmp_pos_v = nrm(ks[4], (L, CMP_LEN, HEAD_DIM), 0.1)
    cmp_w1_k = nrm(ks[5], (L, CMP_LEN * HEAD_DIM, CMP_HIDDEN), (CMP_LEN * HEAD_DIM) ** -0.5)
    cmp_w2_k = nrm(ks[6], (L, CMP_HIDDEN, HEAD_DIM), CMP_HIDDEN ** -0.5)
    cmp_w1_v = nrm(ks[7], (L, CMP_LEN * HEAD_DIM, CMP_HIDDEN), (CMP_LEN * HEAD_DIM) ** -0.5)
    cmp_w2_v = nrm(ks[8], (L, CMP_HIDDEN, HEAD_DIM), CMP_HIDDEN ** -0.5)
    g_out = 1.0 + nrm(ks[9], (L, D_MIX), 0.02)
    w_out = nrm(ks[10], (L, D_MIX, D_MODEL), D_MIX ** -0.5 * DEEPNORM_BETA)
    ln1_g = 1.0 + nrm(ks[11], (L, D_MODEL), 0.02)
    ln1_b = nrm(ks[12], (L, D_MODEL), 0.02)
    router_w = nrm(ks[13], (L, D_MODEL, N_EXPERTS), D_MODEL ** -0.5)
    router_b = nrm(ks[14], (L, N_EXPERTS), 0.01)
    w_gate_up = nrm(ks[15], (L, N_EXPERTS, D_MODEL, 2 * D_EXPERT), D_MODEL ** -0.5)
    b_gate_up = nrm(ks[16], (L, N_EXPERTS, 2 * D_EXPERT), 0.01)
    w_down = nrm(ks[17], (L, N_EXPERTS, D_EXPERT, D_MODEL), D_EXPERT ** -0.5 * DEEPNORM_BETA)
    b_down = nrm(ks[18], (L, N_EXPERTS, D_MODEL), 0.01)
    ln2_g = 1.0 + nrm(ks[19], (L, D_MODEL), 0.02)
    ln2_b = nrm(ks[20], (L, D_MODEL), 0.02)
    return {'x': x, 'w_in': w_in, 'b_in': b_in, 'cmp_pos_k': cmp_pos_k, 'cmp_pos_v': cmp_pos_v,
            'cmp_w1_k': cmp_w1_k, 'cmp_w2_k': cmp_w2_k, 'cmp_w1_v': cmp_w1_v, 'cmp_w2_v': cmp_w2_v,
            'g_out': g_out, 'w_out': w_out, 'ln1_g': ln1_g, 'ln1_b': ln1_b,
            'router_w': router_w, 'router_b': router_b, 'w_gate_up': w_gate_up, 'b_gate_up': b_gate_up,
            'w_down': w_down, 'b_down': b_down, 'ln2_g': ln2_g, 'ln2_b': ln2_b}

def reference(x, w_in, b_in, cmp_pos_k, cmp_pos_v, cmp_w1_k, cmp_w2_k, cmp_w1_v, cmp_w2_v,
              g_out, w_out, ln1_g, ln1_b, router_w, router_b, w_gate_up, b_gate_up,
              w_down, b_down, ln2_g, ln2_b):
    for l in range(DEPTH):
        mix = hybrid_mixer(x, w_in[l], b_in[l], cmp_pos_k[l], cmp_pos_v[l], cmp_w1_k[l], cmp_w2_k[l],
                           cmp_w1_v[l], cmp_w2_v[l], g_out[l], w_out[l])
        x = layer_norm(DEEPNORM_ALPHA * x + mix, ln1_g[l], ln1_b[l])
        ffn = moe_ffn(x, router_w[l], router_b[l], w_gate_up[l], b_gate_up[l], w_down[l], b_down[l])
        x = layer_norm(DEEPNORM_ALPHA * x + ffn, ln2_g[l], ln2_b[l])
    return x


_drawn_inputs = setup_inputs


def setup_inputs(seed=0):
    import zlib

    import numpy as np

    out = dict(_drawn_inputs(seed))
    spreads = {}
    factors = {'cmp_pos_k': 5.325,
     'g_out': 3.272,
     'router_b': 3.138,
     'b_gate_up': 8.0,
     'b_down': 8.0,
     'ln2_g': 2.836,
     'ln2_b': 2.949}
    for name, (base, spread) in spreads.items():
        noise = np.random.default_rng([zlib.crc32(name.encode()), seed]).standard_normal(out[name].shape)
        drawn = base * np.exp(spread * noise) if base else spread * noise
        out[name] = __import__('jax').numpy.asarray(drawn.astype(out[name].dtype))
    for name, factor in factors.items():
        out[name] = (out[name] * factor).astype(out[name].dtype)
    return out
```

```python
from contextlib import ExitStack

import concourse.bass as bass
from concourse import mybir

ALU = mybir.AluOpType
ACT = mybir.ActivationFunctionType
AX = mybir.AxisListType
F32 = mybir.dt.float32
BF16 = mybir.dt.bfloat16
U32 = mybir.dt.uint32
I32 = mybir.dt.int32

P = 128
TOKENS = 256
TB = TOKENS // P
D = 1024
KT = D // P
DH = 64
CMP_LEN, CMP_STRIDE, CMP_BLOCKS = 32, 16, 16
N_EXPERTS = 32
TOP_K = 4
PAIRS = N_EXPERTS // 2
SLOTS = 64
EXPERTS_PADDED = N_EXPERTS + 2
GU_CHUNKS = 4
DN_CHUNKS = 4
ALPHA = 2.0 ** 0.25
SCALE = DH ** -0.5
LN_EPS, RMS_EPS = 1e-5, 1e-6
LIMIT, SWIGLU_ALPHA = 7.0, 1.702
MASKED = -1e30
NOT_ROUTED = -4096.0
N_ROWS, G_OUT_COL = 57, 49
GELU_C = 0.7978845608028654

C_Q, C_KC, C_VC, C_KS, C_VS, C_KW, C_VW, C_GATE = 0, 512, 640, 768, 896, 1024, 1152, 1280
C_FQ, C_FK, C_FV, C_FF, C_BQ, C_BK, C_BV, D_IN = 1304, 1560, 1816, 2072, 2076, 2332, 2588, 2844
V_SEL, V_WIN, V_GATE, V_FOX, V_F, V_SB, V_COLS = 0, 128, 256, 280, 536, 540, 796


W_IN_GROUPS = [(C_KC, C_KS), (C_KS, C_FQ), (0, C_KC), (C_FQ, C_BQ), (C_BQ, D_IN)]


def slope(head):
    return 2.0 ** (-8.0 * (head + 1) / 8)


def hybrid_layer(nc, x, w_in, b_in, pos_k, pos_v, w1_k, w2_k, w1_v, w2_v, g_out, w_out, ln1_g, ln1_b,
                 router_w, router_b, w_gu, b_gu, w_dn, b_dn, ln2_g, ln2_b, out):
    with ExitStack() as ctx:
        def sb(name, cols, dt=F32):
            return ctx.enter_context(nc.sbuf_tensor(name, [P, cols], dt))

        def sem(name):
            return ctx.enter_context(nc.semaphore(name))

        GU = KT * 2 * D
        WB = sb("WB", 2 * GU + KT * D)
        reg_b, reg_a, reg_dn = WB[:, 0:GU], WB[:, GU:2 * GU], WB[:, 2 * GU:2 * GU + KT * D]
        gu_slot = [reg_a.rearrange("p (k n) -> p k n", k=KT), reg_b.rearrange("p (k n) -> p k n", k=KT)]
        dn_slot = reg_dn.rearrange("p (k n) -> p k n", k=KT)
        w_in_sb = WB[:, GU:GU + KT * D_IN].rearrange("p (k n) -> p k n", k=KT)
        wo_sb = dn_slot

        def carver(region):
            at = [0]

            def take(cols, **shape):
                a = region[:, at[0]:at[0] + cols]
                at[0] += cols
                if shape:
                    names = " ".join(shape)
                    a = a.rearrange(f"p ({names}) -> p {names}", **shape)
                return a
            return take

        X = sb("X", TB * D)
        x_sb = X[:, :].rearrange("p (b d) -> p b d", b=TB)
        S1 = sb("S1", KT * TOKENS)
        oT = S1[:, :].rearrange("p (k t) -> p k t", k=KT)
        bgu = S1[:, :]
        S2 = sb("S2", 6656)
        take = carver(S2[:, :])
        x1T = take(KT * TOKENS, k=KT, t=TOKENS)
        xT = x1T
        y = take(TB * D, b=TB, d=D)
        lng = take(D)
        lnb = take(D)
        rw = take(KT * N_EXPERTS, k=KT, e=N_EXPERTS)
        take = carver(S2[:, KT * TOKENS:])
        alibi = take(8 * 384, h=8, k=384)
        causal = take(384)
        dist = take(384)
        take = carver(S2[:, :])
        xg = take(KT * 2 * SLOTS, k=KT, s=2 * SLOTS)
        gt = take(512)
        ut = take(512)
        act_sb = take(512)
        actT = take(512, c=4, s=P)
        ysb = take(1024, n=2, d=512)
        actTx = take(512, c=4, s=P)
        xgx = take(KT * SLOTS, k=KT, s=SLOTS)
        CTx = take(TB * P, b=TB, t=P)
        ohwx = take(TB * P, b=TB, s=P)
        ohx = take(TB * SLOTS, b=TB, s=SLOTS)
        ohw = take(TB * P, b=TB, s=P)
        CT = take(TB * P, b=TB, t=P)
        oh = take(TB * P, b=TB, s=P)
        sel = take(2 * SLOTS, e=2, s=SLOTS)
        yx = xgx.rearrange("p k s -> p (k s)")
        yf = S2[:, 0:TB * D].rearrange("p (b d) -> p b d", b=TB)
        fg, fb = reg_a[:, 0:D], reg_a[:, D:2 * D]

        K = sb("K", 1170)
        take = carver(K[:, :])
        ident = take(P)
        iota_s = take(SLOTS)
        pidx = take(SLOTS)
        posm = take(EXPERTS_PADDED * TB, e=EXPERTS_PADDED, b=TB)
        wts = take(EXPERTS_PADDED * TB, e=EXPERTS_PADDED, b=TB)
        lg = take(TB * N_EXPERTS, b=TB, e=N_EXPERTS)
        msk = take(TB * N_EXPERTS, b=TB, e=N_EXPERTS)
        m8 = take(TB * 8, b=TB, e=8)
        oh4 = take(TB * 4 * N_EXPERTS, b=TB, e=N_EXPERTS, k=4)
        st = take(TB * 12 + 4 * TB)
        rb = take(N_EXPERTS)
        rms = take(8)
        half = take(8)
        curp = take(4)
        curw = take(4)
        curx = take(2)
        xw = take(2)
        ecnt = take(2)
        row1 = take(16)
        before = take(2 * P)
        idx8 = sb("idx8", TB * 8, U32)
        nx = sb("nx", EXPERTS_PADDED, I32)
        idx4f = sb("idx4f", TB * 4)

        take = carver(reg_b)
        qn = take(4 * TOKENS, r=4, t=TOKENS)
        kzs = take(512, g=2, t=TOKENS)
        kzw = take(512, g=2, t=TOKENS)
        fq = take(512, j=2, t=TOKENS)
        fkz = take(1024, j=2, h=2, t=TOKENS)
        bk = take(512, j=2, t=TOKENS)
        bqz = take(1024, j=2, h=2, t=TOKENS)
        V = take(TB * V_COLS, b=TB, c=V_COLS)
        kv2 = [take(576, g=2, t=288) for _ in range(2)]
        kvp = [[take(288) for _ in range(2)] for _ in range(2)]
        w1 = [take(2048, j=16, n=P) for _ in range(2)]
        bV = take(V_COLS)
        le_ones = take(256)
        neg_ge = take(P)
        take_b = take
        take = carver(reg_a)
        fbias = take(4 * 384, h=4, k=384)
        strict_add = take(768)
        strict_01 = take(768)
        L = [take(768) for _ in range(3)]
        PT = [take(768) for _ in range(2)]
        lfb = take(TB * 4 * P, b=TB, h=4, q=P)
        zc = [take(768) for _ in range(2)]
        sp = [take(768) for _ in range(2)]
        zm = [take(768) for _ in range(2)]
        sq = take(256)
        ssq = take(3 * 256, g=3, t=TOKENS)
        hx = take(P)
        h2 = take(P)
        hu = take(P)
        hidT = take(64)
        hidV = take(P)
        kcz = take(32)
        VCZ = take(512, h=8, d=DH)
        Lc = take(256)
        PcT = take(256)
        cb = take(256, b=TB, h=8, n=16)
        dc = take(32, b=TB, n=16)
        vmask = take(8)
        cm = take(32, b=TB, n=16)
        take = take_b
        w2sb = take(2 * DH)
        rows = take(P)
        cols = take(N_ROWS)
        posT = cols[:, 0:32]
        mx = [take(4) for _ in range(3)]
        nmx = [take(4) for _ in range(3)]
        sm = [take(4) for _ in range(3)]
        rr = [take(4) for _ in range(3)]
        gs = take(TB * 24, b=TB, c=24)
        avail = take(2)
        lf = take(TB * 4, b=TB, h=4)
        lt = take(TB * 4, b=TB, h=4)
        ncq = take(TB * 4, b=TB, h=4)
        cmx = take(16)
        csm = take(16)
        ones1 = take(1)
        PB = [ctx.enter_context(nc.psum_tensor(f"PB{i}", [P, 512], F32)) for i in range(8)]

        names = """x_in smalls rows_ld rows_ps bv_ld w1ld wo_ld ln_ld ln2_ld bdn_ld bgu_ld cst zer xt_ps xt_sb proj ev_dve ev_act
        kvp_ok hid hid_dve hid_act hidt hidt_sb kcv kcv_sb csc cexp_in cexp pc pct pct_sb logf lf_dve lf_act
        clq clq_sb fb_ps fb_ok tables masks sc ttr exp scaled pts pta ptb pv sqs oscaled ssq_acc
        zs zcp zabs sps zmk spm incl arg aexp ssqm rms_in rms_p rms_ok op ymix lnstat lnp lnok x1ok x1t x1tsb lgt
        route ract rsum cntp routed xin ysz ysb_ok clip upg cur cse xclip xupg xcur wt_ps wt_sb accinit xa
        ohs oht ga xg_ok guc g_ok sig act at actT dn_used ct ct_sb comb xsec
        xoh xga xxg xct xctd xguc xdnc xgok xsig xact xat xactT xyd fin flnp fout outd v_self a_self p_self""".split()
        s = {n: sem("s_" + n) for n in names}
        s_win = [sem(f"s_win{i}") for i in range(5)]
        s_gul = [[sem(f"s_gul{e}{c}") for c in range(GU_CHUNKS)] for e in range(2)]
        s_dnl = [[sem(f"s_dnl{e}{c}") for c in range(DN_CHUNKS)] for e in range(2)]
        block = ctx.enter_context(nc.Block())

        feat = [("kc", C_KC, 0), ("vc", C_VC, 0), ("ks", C_KS, 1), ("kw", C_KW, 1),
                ("q0", 0, 2), ("q1", 1, 2), ("q2", 2, 2), ("q3", 3, 2),
                ("fq0", C_FQ, 3), ("fq1", C_FQ + P, 3), ("fk0", C_FK, 3), ("fk1", C_FK + P, 3),
                ("bq0", C_BQ, 4), ("bq1", C_BQ + P, 4), ("bk0", C_BK, 4), ("bk1", C_BK + P, 4)]
        toks = {"vs": (C_VS, 128, V_SEL, 1), "vw": (C_VW, 152, V_WIN, 1), "vf": (C_FV, 260, V_FOX, 3),
                "vb": (C_BV, 256, V_SB, 4)}
        outputs = [f[0] for f in feat[:4]] + ["vs.0", "vs.1", "vw.0", "vw.1"] + [f[0] for f in feat[4:12]] + \
                  ["vf.0", "vf.1"] + [f[0] for f in feat[12:]] + ["vb.0", "vb.1"]
        fdict = {f[0]: f for f in feat}
        bcol = {"kc": 32, "vc": 33, "ks": 34, "kw": 36, "q0": 37, "q1": 38, "q2": 39, "q3": 40, "fq0": 41, "fq1": 42,
                "fk0": 43, "fk1": 44, "bq0": 45, "bq1": 46, "bk0": 47, "bk1": 48}
        by_act = {"kc", "vc", "ks", "kw", "fk0", "fk1", "bk0", "bk1"}
        ready, n_dve, n_act = {}, 0, 0
        for o in outputs:
            if o in by_act:
                n_act += 1
                ready[o] = ("ev_act", n_act)
            else:
                n_dve += 1
                ready[o] = ("ev_dve", n_dve)
        units = [(b, r) for r in range(4) for b in ("sel", "win")] + [("fox", 0), ("fox", 1)]
        NU = len(units)
        o_order = [("nsa", r) for r in range(4)] + [("fox", 0), ("fox", 1), ("sb", 0), ("sb", 1)]
        o_index = {k: i for i, k in enumerate(o_order)}

        def need(eng, what):
            n, v = ready[what]
            eng.wait_ge(s[n], v)

        def chain(eng, name):
            n = [0]

            def link(ins):
                n[0] += 1
                ins.then_inc(s[name], 1)
                eng.wait_ge(s[name], n[0])
            return link

        @block.sync
        def _(sp_):
            sp = sp_
            sp.dma_start(x_sb, x[0].rearrange("(b p) d -> p b d", p=P)).then_inc(s["x_in"], 16)
            w_v = w_in[0].rearrange("(k p) n -> p k n", p=P)
            for dst, src in ((rows[0:16, :], pos_k[0].rearrange("(j a) d -> j (a d)", a=2)),
                             (rows[16:32, :], pos_v[0].rearrange("(j a) d -> j (a d)", a=2)),
                             (rows[32:37, :], b_in[0, C_KC:C_KC + 5 * P].rearrange("(r n) -> r n", n=P)),
                             (rows[37:41, :].rearrange("r (g d) -> r g d", g=2),
                              b_in[0, 0:C_KC].rearrange("(g r d) -> r g d", g=2, r=4)),
                             (rows[41:45, :], b_in[0, C_FQ:C_FQ + 4 * P].rearrange("(r n) -> r n", n=P)),
                             (rows[45:49, :], b_in[0, C_BQ:C_BQ + 4 * P].rearrange("(r n) -> r n", n=P)),
                             (rows[49:53, :].rearrange("r (g d) -> r g d", g=2),
                              g_out[0, 0:512].rearrange("(g r d) -> r g d", g=2, r=4)),
                             (rows[53:57, :], g_out[0, 512:D].rearrange("(r n) -> r n", n=P))):
                sp.dma_start(dst, src).then_inc(s["rows_ld"], 16)
            for i, (a, b) in enumerate(W_IN_GROUPS):
                sp.dma_start(w_in_sb[:, :, a:b], w_v[:, :, a:b]).then_inc(s_win[i], 16)
                if i == 0:
                    for c, n, at, _ in toks.values():
                        sp.dma_start(bV[:, at:at + n], b_in[0:1, c:c + n].broadcast_to([P, n])).then_inc(s["bv_ld"], 16)
            for i, w in enumerate((w1_k, w1_v)):
                sp.dma_start(w1[i], w[0].rearrange("(j p) n -> p j n", p=P)).then_inc(s["w1ld"], 16)
            sp.wait_ge(s["proj"], len(outputs))
            for g in range(2):
                sp.dma_start(wo_sb[64 * g:64 * g + 64, 0:4, :],
                             w_out[0, 256 * g:256 * g + 256, :].rearrange("(r p) n -> p r n", p=DH)).then_inc(s["wo_ld"], 16)
            sp.dma_start(wo_sb[:, 4:8, :], w_out[0, 512:1024, :].rearrange("(r p) n -> p r n", p=P)).then_inc(s["wo_ld"], 16)
            sp.wait_ge(s["pv"], NU + 2)
            sp.wait_ge(s["ssqm"], 6)
            sp.wait_ge(s["oscaled"], 8)
            sp.wait_ge(s["rms_in"], 1)
            for t, src in ((lng, ln1_g), (lnb, ln1_b)):
                sp.dma_start(t, src[0:1, :].broadcast_to([P, D])).then_inc(s["ln_ld"], 16)
            sp.dma_start(rw, router_w[0].rearrange("(k p) e -> p k e", p=P)).then_inc(s["ln_ld"], 16)

            gu_v = w_gu[0].rearrange("e (k p) n -> e p k n", p=P)
            dn_v = w_dn[0].rearrange("e (k p) n -> e p k n", p=P)

            def load_gu(i, par, c):
                kk = KT // GU_CHUNKS
                src = gu_v[2 * i + par] if isinstance(i, int) else gu_v[bass.ds(2 * i + par, 1)].rearrange("e p k n -> (e p) k n")
                sp.dma_start(gu_slot[par][:, kk * c:kk * c + kk, :], src[:, kk * c:kk * c + kk, :]).then_inc(s_gul[par][c], 16)

            def load_dn(i, par, c):
                kk = KT // DN_CHUNKS
                src = dn_v[2 * i + par] if isinstance(i, int) else dn_v[bass.ds(2 * i + par, 1)].rearrange("e p k n -> (e p) k n")
                sp.dma_start(dn_slot[:, kk * c:kk * c + kk, :], src[:, kk * c:kk * c + kk, :]).then_inc(s_dnl[par][c], 16)

            def count_extra_blocks(e):
                n = sp.value_load(nx[0:1, e:e + 1] if isinstance(e, int) else nx[0:1, bass.ds(e, 1)], min_val=0, max_val=3)
                sp.reg_add(xcount, xcount, n)

            def use_by_extra_blocks(c):
                return sp.snap(sp.snap(xcount, min_val=0, max_val=96) * 4 + (c + 1), min_val=1, max_val=4 * 97)

            xcount = sp.alloc_register("sp_extra_blocks")
            sp.reg_mov(xcount, 0)
            for par in range(2):
                for c in range(GU_CHUNKS):
                    load_gu(0, par, c)
            sp.wait_ge(s["op"], 12)
            for c in range(DN_CHUNKS):
                load_dn(0, 0, c)
            sp.wait_ge(s["routed"], 1)
            with sp.Fori(0, PAIRS - 1) as i:
                for par in range(2):
                    count_extra_blocks(2 * i + par)
                    for c in range(GU_CHUNKS):
                        xc = use_by_extra_blocks(c)
                        sp.wait_ge(s["guc"], i * (2 * GU_CHUNKS) + (par * GU_CHUNKS + c + 1))
                        sp.wait_ge(s["xguc"], xc)
                        load_gu(i + 1, par, c)
                    for c in range(DN_CHUNKS):
                        xc = use_by_extra_blocks(c)
                        sp.wait_ge(s["dn_used"], i * (2 * DN_CHUNKS) + (par * DN_CHUNKS + c + 1))
                        sp.wait_ge(s["xdnc"], xc)
                        load_dn(i + par, 1 - par, c)
            count_extra_blocks(N_EXPERTS - 2)
            for c in range(DN_CHUNKS):
                xc = use_by_extra_blocks(c)
                sp.wait_ge(s["dn_used"], (N_EXPERTS - 2) * DN_CHUNKS + c + 1)
                sp.wait_ge(s["xdnc"], xc)
                load_dn(PAIRS - 1, 1, c)
            sp.wait_ge(s["guc"], N_EXPERTS * GU_CHUNKS)
            for t, src in ((fg, ln2_g), (fb, ln2_b)):
                sp.dma_start(t, src[0:1, :].broadcast_to([P, D])).then_inc(s["ln2_ld"], 16)
            for b in range(TB):
                sp.wait_ge(s["fout"], b + 1)
                sp.dma_start(out[0, P * b:P * b + P, :], yf[:, b, :]).then_inc(s["outd"], 16)
            sp.wait_ge(s["outd"], 16 * TB)

        @block.gpsimd
        def _(pool):
            link = chain(pool, "p_self")
            sel_op = pool.affine_select
            link(pool.memset(ident, 0.0))
            sel_op(out=ident, in_=ident, compare_op=ALU.not_equal, fill=1.0, base=0, pattern=[[-1, P]],
                   channel_multiplier=1).then_inc(s["cst"], 1)
            link(pool.memset(causal, 0.0))
            link(sel_op(out=causal[:, 0:P], in_=causal[:, 0:P], compare_op=ALU.is_ge, fill=MASKED, base=0,
                        pattern=[[-1, P]], channel_multiplier=1))
            sel_op(out=causal[:, P:384], in_=causal[:, P:384], compare_op=ALU.is_ge, fill=MASKED, base=P,
                   pattern=[[-1, 256]], channel_multiplier=1).then_inc(s["tables"], 1)
            pool.iota(dist[:, 0:P], [[1, P]], base=0, channel_multiplier=-1,
                      allow_small_or_imprecise_dtypes=True).then_inc(s["tables"], 1)
            pool.iota(dist[:, P:384], [[1, 256]], base=-P, channel_multiplier=-1,
                      allow_small_or_imprecise_dtypes=True).then_inc(s["tables"], 1)
            for t in (kzs, kzw, fkz, bqz, kv2[0], kv2[1]):
                pool.memset(t, 0.0).then_inc(s["zer"], 1)
            link(pool.memset(le_ones, -1.0))
            sel_op(out=le_ones[:, 0:P], in_=le_ones[:, 0:P], compare_op=ALU.is_ge, fill=0.0, base=0,
                   pattern=[[1, P]], channel_multiplier=-1).then_inc(s["tables"], 1)
            link(pool.memset(neg_ge, -1.0))
            sel_op(out=neg_ge, in_=neg_ge, compare_op=ALU.is_ge, fill=0.0, base=0,
                   pattern=[[-1, P]], channel_multiplier=1).then_inc(s["tables"], 1)
            pool.iota(iota_s, [[1, SLOTS]], base=0, channel_multiplier=0,
                      allow_small_or_imprecise_dtypes=True).then_inc(s["tables"], 1)
            pool.iota(pidx, [[0, SLOTS]], base=0, channel_multiplier=1,
                      allow_small_or_imprecise_dtypes=True).then_inc(s["tables"], 1)
            link(pool.memset(avail, 1.0))
            sel_op(out=avail[:, 0:1], in_=avail[:, 0:1], compare_op=ALU.is_ge, fill=0.0, base=-(CMP_LEN - 1),
                   pattern=[[0, 1]], channel_multiplier=1).then_inc(s["tables"], 1)
            pool.memset(half, -0.5).then_inc(s["tables"], 1)
            pool.memset(ones1, 1.0).then_inc(s["tables"], 1)
            link(pool.memset(before, 1.0))
            sel_op(out=before[:, 0:P], in_=before[:, 0:P], compare_op=ALU.is_ge, fill=0.0, base=-1,
                   pattern=[[1, P]], channel_multiplier=-1).then_inc(s["tables"], 1)
            pool.wait_ge(s["proj"], len(outputs))
            pool.iota(dc, [[-P, TB], [CMP_STRIDE, 16]], base=CMP_LEN - 1, channel_multiplier=-1,
                      allow_small_or_imprecise_dtypes=True).then_inc(s["masks"], 1)
            link(pool.memset(vmask, 1.0))
            link(sel_op(out=vmask, in_=vmask, compare_op=ALU.is_ge, fill=0.0, base=0, pattern=[[-16, 8]],
                        channel_multiplier=1))
            sel_op(out=vmask, in_=vmask, compare_op=ALU.is_ge, fill=0.0, base=15, pattern=[[16, 8]],
                   channel_multiplier=-1).then_inc(s["masks"], 1)
            pool.memset(kcz, 0.0).then_inc(s["masks"], 1)
            link(pool.memset(cm, 0.0))
            sel_op(out=cm, in_=cm, compare_op=ALU.is_ge, fill=MASKED, base=-(CMP_LEN - 1),
                   pattern=[[P, TB], [-CMP_STRIDE, 16]], channel_multiplier=1).then_inc(s["masks"], 1)
            for t, base, fill in ((strict_add, 0.0, MASKED), (strict_01, 1.0, 0.0)):
                link(pool.memset(t, base))
                link(sel_op(out=t[:, 0:512], in_=t[:, 0:512], compare_op=ALU.is_ge, fill=fill, base=-1,
                            pattern=[[0, 2], [1, 256]], channel_multiplier=-1))
                sel_op(out=t[:, 512:768], in_=t[:, 512:768], compare_op=ALU.is_ge, fill=fill, base=-1,
                       pattern=[[0, 2], [1, P]], channel_multiplier=-1).then_inc(s["masks"], 1)
            for j in range(2):
                pool.wait_ge(s["zcp"], j + 1)
                if j == 0:
                    pool.wait_ge(s["masks"], 6)
                pool.tensor_tensor(zm[j], zc[j], strict_add, ALU.add).then_inc(s["zmk"], 1)
            pool.wait_ge(s["rms_in"], 1)
            pool.tensor_tensor(rms[:, 0:6], rms[:, 0:6], half[:, 0:6], ALU.pow).then_inc(s["rms_p"], 1)
            for b in range(TB):
                pool.wait_ge(s["lnstat"], b + 1)
                pool.tensor_tensor(st[:, 24 + 4 * b + 2:24 + 4 * b + 3], st[:, 24 + 4 * b + 1:24 + 4 * b + 2],
                                   half[:, 0:1], ALU.pow).then_inc(s["lnp"], 1)
            for b in range(TB):
                pool.wait_ge(s["fin"], b + 1)
                pool.tensor_tensor(st[:, 24 + 4 * b + 2:24 + 4 * b + 3], st[:, 24 + 4 * b + 1:24 + 4 * b + 2],
                                   half[:, 0:1], ALU.pow).then_inc(s["flnp"], 1)

        @block.scalar
        def _(act):
            link = chain(act, "a_self")

            for dst, src in ((w2sb[:, 0:DH], w2_k[0]), (w2sb[:, DH:2 * DH], w2_v[0]),
                             (rb, router_b[0:1, :].broadcast_to([P, N_EXPERTS]))):
                act.dma_start(dst, src).then_inc(s["smalls"], 16)

            for b in (1, 3):
                act.wait_ge(s["xt_ps"], b + 1)
                act.activation(xT[:, 2 * b:2 * b + 2, :].rearrange("p k t -> p (k t)"), PB[b][:, :], ACT.Copy)\
                   .then_inc(s["xt_sb"], 1)
            act.wait_ge(s["kvp_ok"], 1)
            act.wait_ge(s["zer"], 6)

            def bias_copy(dst, src, name, p0, p1):
                return act.activation(dst, src, ACT.Identity, bias=cols[p0:p1, bcol[name]:bcol[name] + 1])

            for n, name in enumerate(outputs):
                if name not in by_act:
                    continue
                act.wait_ge(s["proj"], n + 1)
                ps = PB[n % 8]
                if name in ("kc", "vc"):
                    d = kv2[0 if name == "kc" else 1]
                    bias_copy(d[0:64, 0, 0:256], ps[0:64, 0:256], name, 0, 64)
                    bias_copy(d[64:128, 1, 0:255], ps[64:128, 1:256], name, 64, 128)
                    bias_copy(d[64:128, 0, 0:255], ps[0:64, 1:256], name, 0, 64)
                    bias_copy(d[0:64, 1, 0:256], ps[64:128, 0:256], name, 64, 128).then_inc(s["ev_act"], 1)
                elif name in ("bk0", "bk1"):
                    bias_copy(bk[:, int(name[-1]), :], ps[:, 0:256], name, 0, 128).then_inc(s["ev_act"], 1)
                else:
                    d = {"ks": kzs, "kw": kzw, "fk0": fkz[:, 0], "fk1": fkz[:, 1]}[name]
                    bias_copy(d[0:64, 0, :], ps[0:64, 0:256], name, 0, 64)
                    bias_copy(d[64:128, 1, :], ps[64:128, 0:256], name, 64, 128).then_inc(s["ev_act"], 1)
            act.wait_ge(s["hid_dve"], 1)
            act.activation(hu[0:64, :], hu[0:64, :], ACT.Tanh).then_inc(s["hid_act"], 1)
            act.wait_ge(s["lf_dve"], 1)
            link(act.activation(gs, gs, ACT.Exp, scale=-1.0))
            link(act.activation(lt, V[:, :, V_F:V_F + 4], ACT.Abs))
            link(act.activation(lt, lt, ACT.Exp, scale=-1.0))
            act.activation(lt, lt, ACT.Ln, bias=1.0).then_inc(s["lf_act"], 1)
            act.wait_ge(s["cexp_in"], 1)
            act.activation(Lc, Lc, ACT.Exp).then_inc(s["cexp"], 1)
            act.wait_ge(s["pct"], 1)
            act.activation(PcT, PB[4][:, 0:256], ACT.Copy).then_inc(s["pct_sb"], 1)

            def exps(u):
                act.wait_ge(s["ttr"], u + 1)
                l = L[u % 3]
                for c, (a, b) in enumerate(((0, 128), (128, 256), (256, 512), (512, 768))):
                    ins = act.activation(l[:, a:b], l[:, a:b], ACT.Exp, bias=nmx[u % 3][:, c:c + 1],
                                         accum_out=sm[u % 3][:, c:c + 1])
                ins.then_inc(s["exp"], 1)

            def pta(u):
                act.wait_ge(s["pts"], 2 * u + 1)
                if u >= 2:
                    act.wait_ge(s["pv"], u - 1)
                act.activation(PT[u % 2][:, 0:384], PB[4][:, 0:384], ACT.Copy).then_inc(s["pta"], 1)

            def squares(i):
                kind, r = o_order[i]
                last = {"nsa": 2 * r + 2, "fox": 9 + r, "sb": NU + 1 + r}[kind]
                act.wait_ge(s["pv"], last)
                ps = PB[6 + i % 2][:, 0:256]
                g = {"nsa": 0, "fox": 1, "sb": 2}[kind]
                first = r == 0
                if not first:
                    act.wait_ge(s["ssq_acc"], sum(1 for k, rr_ in o_order[:i] if rr_ > 0))
                link(act.activation(ssq[:, g, :] if first else sq, ps, ACT.Square))
                act.activation(oT[:, i, :], ps, ACT.Copy, scale=cols[:, G_OUT_COL + i:G_OUT_COL + i + 1]).then_inc(s["oscaled"], 1)

            for t in range(NU + 3):
                if t < NU:
                    exps(t)
                if 2 <= t < NU + 2:
                    pta(t - 2)
                u = t - 3
                if u >= 0:
                    if units[u][0] == "win":
                        squares(o_index[("nsa", units[u][1])])
                    elif units[u][0] == "fox":
                        squares(o_index[units[u]])
            for j in range(2):
                act.wait_ge(s["zcp"], j + 1)
                link(act.activation(sp[j], zc[j], ACT.Abs))
            for j in range(2):
                link(act.activation(sp[j], sp[j], ACT.Exp, scale=-1.0))
            for j in range(2):
                act.activation(sp[j], sp[j], ACT.Ln, bias=1.0).then_inc(s["sps"], 1)
            for j in range(2):
                act.wait_ge(s["arg"], j + 1)
                act.activation(zm[j], zm[j], ACT.Exp).then_inc(s["aexp"], 1)
            for j in range(2):
                squares(6 + j)

            act.wait_ge(s["op"], 12)
            act.dma_start(bgu[0:N_EXPERTS, :], b_gu[0]).then_inc(s["bgu_ld"], 16)
            for b in range(TB):
                for h in range(2):
                    act.wait_ge(s["x1t"], 2 * b + h + 1)
                    act.activation(x1T[:, 4 * h:4 * h + 4, P * b:P * b + P],
                                   PB[4 + 2 * b + h][:, :].rearrange("p (k t) -> p k t", k=4), ACT.Copy)\
                       .then_inc(s["x1tsb"], 1)
            for b in range(TB):
                act.wait_ge(s["ract"], b + 1)
                act.activation(lg[:, b, :], lg[:, b, :], ACT.Exp).then_inc(s["rsum"], 1)
            act.wait_ge(s["ysz"], 1)
            act.dma_start(ysb[0:N_EXPERTS, :, :], b_dn[0].rearrange("e (h d) -> e h d", h=2)).then_inc(s["bdn_ld"], 16)
            act.wait_ge(s["wt_ps"], 1)
            act.wait_ge(s["ysz"], 2)
            act.activation(CT[0:N_EXPERTS, :, :].rearrange("p b t -> p (b t)"), PB[4][0:N_EXPERTS, 0:256],
                           ACT.Copy).then_inc(s["ysb_ok"], 1)

            def slots_to_sbuf(h, n):
                act.wait_ge(s["ga"], n)
                act.activation(xg[:, 4 * h:4 * h + 4, :].rearrange("p k s -> p (k s)"), PB[6 + h][:, :], ACT.Copy)\
                   .then_inc(s["xg_ok"], 1)

            slots_to_sbuf(0, 1)
            slots_to_sbuf(1, 2)
            xcount = act.alloc_register("act_extra_blocks")
            act.reg_mov(xcount, 0)

            def extra_slots():
                act.reg_add(xcount, xcount, 1)
                xc = act.snap(xcount, min_val=1, max_val=96)
                act.wait_ge(s["xga"], xc)
                act.activation(xgx[:, :, :].rearrange("p k s -> p (k s)"), PB[6][:, :], ACT.Copy).then_inc(s["xxg"], 1)
                act.wait_ge(s["xct"], xc)
                act.activation(CTx[:, :, :].rearrange("p b t -> p (b t)"), PB[7][:, 0:256], ACT.Copy)\
                   .then_inc(s["xctd"], 1)
                act.wait_ge(s["xgok"], xc)
                act.activation(act_sb, gt, ACT.Sigmoid, scale=SWIGLU_ALPHA).then_inc(s["xsig"], 1)
                act.wait_ge(s["xat"], xc)
                act.activation(actTx[:, :, :].rearrange("p c s -> p (c s)"), PB[6][:, :], ACT.Copy)\
                   .then_inc(s["xactT"], 1)

            def extra_outputs():
                act.wait_ge(s["xdnc"], act.snap(act.snap(xcount, min_val=0, max_val=96) * 4 + DN_CHUNKS, min_val=1, max_val=4 * 97))
                act.activation(yx, PB[7][:, :], ACT.Copy).then_inc(s["xyd"], 1)

            with act.Fori(0, PAIRS) as i:
                for e in range(2):
                    E1 = 2 * i + (e + 1)
                    act.wait_ge(s["g_ok"], E1)
                    act.activation(act_sb, gt, ACT.Sigmoid, scale=SWIGLU_ALPHA).then_inc(s["sig"], 1)
                    if e == 0:
                        act.wait_ge(s["ct"], i + 1)
                        act.activation(CT[:, :, :].rearrange("p b t -> p (b t)"), PB[6][:, 0:256], ACT.Copy)\
                           .then_inc(s["ct_sb"], 1)
                    else:
                        slots_to_sbuf(0, 2 * i + 3)
                        slots_to_sbuf(1, 2 * i + 4)
                    act.wait_ge(s["at"], E1)
                    act.activation(actT[:, :, :].rearrange("p c s -> p (c s)"), PB[6][:, :], ACT.Copy)\
                       .then_inc(s["actT"], 1)
                    n = act.value_load(nx[0:1, bass.ds(2 * i + e, 1)], min_val=0, max_val=3)
                    with act.If(n > 0):
                        extra_slots()
                    act.nop()
                    act.wait_ge(s["dn_used"], E1 * DN_CHUNKS)
                    if e == 0:
                        act.wait_ge(s["comb"], i + 1)
                    act.activation(ysb[64 * e:64 * e + 64, 0, :], PB[7][0:64, :], ACT.Copy)
                    act.activation(ysb[64 * e:64 * e + 64, 1, :], PB[7][64:128, :], ACT.Copy).then_inc(s["ysb_ok"], 1)
                    with act.If(n > 0):
                        extra_outputs()
                    act.nop()
                    with act.If(n > 1):
                        with act.Fori(1, n):
                            extra_slots()
                            extra_outputs()
                    act.nop()

        @block.tensor
        def _(pe):
            mm_, tr = pe.matmul, pe.transpose

            def mm(o, l, r, start, stop):
                return mm_(o, l, r, start=start, stop=stop, skip_group_check=True)

            pe.wait_ge(s["x_in"], 16)
            pe.wait_ge(s["cst"], 1)
            for b4 in range(4):
                for k in (2 * b4, 2 * b4 + 1):
                    for b in range(TB):
                        ins = tr(PB[b4][:, (k % 2) * 256 + P * b:(k % 2) * 256 + P * b + P],
                                 x_sb[:, b, P * k:P * k + P], ident)
                ins.then_inc(s["xt_ps"], 1)
            pe.wait_ge(s["rows_ld"], 16 * 8)
            tr(PB[7][:, 0:N_ROWS], rows[0:N_ROWS, :], ident[0:N_ROWS, 0:N_ROWS]).then_inc(s["rows_ps"], 1)
            pe.wait_ge(s["xt_sb"], 4)
            for n, name in enumerate(outputs):
                base = name.split(".")[0]
                grp = fdict[base][2] if base in fdict else toks[base][3]
                pe.wait_ge(s_win[grp], 16)
                if n >= 8:
                    need(pe, outputs[n - 8])
                if n == 7:
                    pe.wait_ge(s["kvp_ok"], 1)
                ps = PB[n % 8]
                for k in range(KT):
                    if base in fdict:
                        c = fdict[base][1]
                        if base[0] == "q":
                            for g in range(2):
                                h0 = DH * (4 * g + c)
                                ins = mm(ps[64 * g:64 * g + 64, 0:256], w_in_sb[:, k, h0:h0 + DH], xT[:, k, :],
                                         k == 0, k == KT - 1)
                        else:
                            ins = mm(ps[:, 0:256], w_in_sb[:, k, c:c + P], xT[:, k, :], k == 0, k == KT - 1)
                    else:
                        c, w_, _, _ = toks[base]
                        b = int(name[-1])
                        ins = mm(ps[:, 0:w_], xT[:, k, P * b:P * b + P], w_in_sb[:, k, c:c + w_], k == 0, k == KT - 1)
                ins.then_inc(s["proj"], 1)
            for o in outputs[-8:]:
                need(pe, o)
            pe.wait_ge(s["kvp_ok"], 3)
            pe.wait_ge(s["w1ld"], 32)
            for j in range(16):
                for kv in range(2):
                    t = kvp[kv][j // 8]
                    c = 36 * (j % 8) + 2 * (j // 8)
                    a = t[:, c:c + 32]
                    ins = mm(PB[0][32 * kv:32 * kv + 32, 0:P], a, w1[kv][:, j, :], j == 0, j == 15)
            ins.then_inc(s["hid"], 1)
            pe.wait_ge(s["logf"], 2)
            pe.wait_ge(s["tables"], 11)
            mm(PB[1][:, 0:4], le_ones[:, 0:P], lf[:, 0, :], True, True)
            mm(PB[1][:, 4:8], le_ones[:, P:256], lf[:, 0, :], False, False)
            mm(PB[1][:, 4:8], le_ones[:, 0:P], lf[:, 1, :], False, True).then_inc(s["clq"], 1)
            for h in range(4):
                ps = PB[2 + h // 2][:, 256 * (h % 2):256 * (h % 2) + 256]
                mm(ps, lfb[:, 0, h, :], le_ones, h % 2 == 0, False)
                ins = mm(ps[:, P:256], lfb[:, 1, h, :], le_ones[:, 0:P], False, True)
            ins.then_inc(s["fb_ps"], 1)
            pe.wait_ge(s["hid_dve"], 2)
            tr(PB[4][:, 0:64], hx[0:64, :], ident[0:64, 0:64]).then_inc(s["hidt"], 1)
            pe.wait_ge(s["hidt_sb"], 1)
            pe.wait_ge(s["smalls"], 48)
            mm(PB[5][0:64, 0:32], w2sb[:, 0:DH], hidT[:, 0:32], True, True)
            mm(PB[5][64:128, 0:32], w2sb[:, 0:DH], hidT[:, 0:32], True, True)
            mm(PB[6][:, 0:DH], hidV, w2sb[:, DH:2 * DH], True, True).then_inc(s["kcv"], 1)
            pe.wait_ge(s["kcv_sb"], 1)
            for b in range(TB):
                for r in range(4):
                    ins = mm(PB[7][:, 128 * b + 32 * r:128 * b + 32 * r + 32], qn[:, r, P * b:P * b + P], kcz,
                             b == 0 and r == 0, True)
            ins.then_inc(s["csc"], 1)
            pe.wait_ge(s["pc"], 1)
            for b in range(TB):
                ins = tr(PB[4][:, P * b:P * b + P], Lc[:, P * b:P * b + P], ident)
            ins.then_inc(s["pct"], 1)

            def scores(u):
                kind, r = units[u]
                q, kz = {"sel": (qn, kzs), "win": (qn, kzw), "fox": (fq, fkz[:, r] if kind == "fox" else None)}[kind]
                if u >= 2:
                    pe.wait_ge(s["ttr"], u - 1)
                else:
                    pe.wait_ge(s["fb_ok"], 1)
                b0, b1 = PB[2 * (u % 2)], PB[2 * (u % 2) + 1]
                mm(b0[:, 0:256], q[:, r, 0:P], kz[:, :, 0:P], True, True)
                mm(b1[:, :], q[:, r, P:256], kz[:, :, :], True, True).then_inc(s["sc"], 1)

            def transposes(u):
                pe.wait_ge(s["scaled"], u + 1)
                l = L[u % 3]
                for h in range(2):
                    if u >= 1:
                        pe.wait_ge(s["pta" if h == 0 else "ptb"], u)
                    elif h == 0:
                        pe.wait_ge(s["pct_sb"], 1)
                    tr(PB[4 + h][:, 0:P], l[:, P * h:P * h + P], ident)
                    tr(PB[4 + h][:, P:256], l[:, 256 + 256 * h:384 + 256 * h], ident)
                    tr(PB[4 + h][:, 256:384], l[:, 384 + 256 * h:512 + 256 * h], ident).then_inc(s["pts"], 1)

            def values(u):
                kind, r = units[u]
                i = o_index[("nsa", r)] if kind != "fox" else o_index[(kind, r)]
                ps = PB[6 + i % 2]
                if kind != "win" and i >= 2:
                    pe.wait_ge(s["oscaled"], i - 1)
                pe.wait_ge(s["pta"], u + 1)
                pe.wait_ge(s["ptb"], u + 1)
                for h in range(2):
                    c = {"sel": V_SEL + DH * h, "win": V_WIN + DH * h, "fox": V_FOX + P * r + DH * h}[kind]
                    o = ps[64 * h:64 * h + 64, :]
                    p = PT[u % 2][:, 384 * h:384 * h + 384]
                    mm(o[:, 0:256], V[:, 0, c:c + DH], p[:, 0:256], kind != "win", False)
                    ins = mm(o[:, P:256], V[:, 1, c:c + DH], p[:, 256:384], False, kind == "fox")
                    if kind == "win":
                        ins = mm(o[:, 0:256], VCZ[:, 2 * r + h, :], PcT, False, True)
                ins.then_inc(s["pv"], 1)

            for t in range(NU + 3):
                if t < NU:
                    scores(t)
                if 2 <= t < NU + 2:
                    transposes(t - 2)
                if t >= 3:
                    values(t - 3)
            for j in range(2):
                pe.wait_ge(s["ttr"], NU)
                mm(PB[2 * j][:, 0:256], bk[:, j, P:256], bqz[:, j, :, P:256], True, True)
                mm(PB[2 * j + 1][:, :], bk[:, j, 0:P], bqz[:, j, :, :], True, True).then_inc(s["zs"], 1)
            for j in range(2):
                pe.wait_ge(s["spm"], j + 1)
                v0 = PB[2 * j + 1][:, :].rearrange("p (h t) -> p h t", h=2)
                mm(PB[2 * j + 1][:, :], neg_ge, sp[j][:, 0:512], True, False)
                mm(v0[:, :, P:256], le_ones[:, P:256], sp[j][:, 512:768], False, True)
                mm(PB[2 * j][:, 0:256], neg_ge, sp[j][:, 512:768], True, True).then_inc(s["incl"], 1)
            for j in range(2):
                i = 6 + j
                pe.wait_ge(s["oscaled"], i - 1)
                pe.wait_ge(s["aexp"], j + 1)
                for h in range(2):
                    c = V_SB + P * j + DH * h
                    o = PB[6 + i % 2][64 * h:64 * h + 64, :]
                    mm(o[:, 0:256], V[:, 0, c:c + DH], zm[j][:, 256 * h:256 * h + 256], True, False)
                    ins = mm(o[:, P:256], V[:, 1, c:c + DH], zm[j][:, 512 + P * h:512 + P * h + P], False, True)
                ins.then_inc(s["pv"], 1)
            pe.wait_ge(s["ssq_acc"], 5)
            for g in range(3):
                for b in range(TB):
                    mm(PB[0][:, 2 * g + b:2 * g + b + 1], ssq[:, g, P * b:P * b + P], ones1, g == 0 and b == 0,
                       True).then_inc(s["ssqm"], 1)
            pe.wait_ge(s["wo_ld"], 48)
            pe.wait_ge(s["oscaled"], 8)
            n = 0
            for b in range(TB):
                for h in range(2):
                    for ks in ((0, 1, 2, 3), (4, 5), (6, 7)):
                        bank = PB[1 + n % 6]
                        if n >= 6:
                            pe.wait_ge(s["ymix"], n - 5)
                        for k in ks:
                            ins = mm(bank[:, :], oT[:, k, P * b:P * b + P], wo_sb[:, k, 512 * h:512 * h + 512],
                                     k == ks[0], k == ks[-1])
                        ins.then_inc(s["op"], 1)
                        n += 1
            pe.wait_ge(s["ymix"], 12)
            pe.wait_ge(s["ln_ld"], 48)
            for b in range(TB):
                pe.wait_ge(s["x1ok"], b + 1)
                for h in range(2):
                    for k in range(4):
                        ins = tr(PB[4 + 2 * b + h][:, P * k:P * k + P], x_sb[:, b, P * (4 * h + k):P * (4 * h + k) + P], ident)
                    ins.then_inc(s["x1t"], 1)
            for b in range(TB):
                pe.wait_ge(s["x1tsb"], 2 * b + 2)
                for k in range(KT):
                    ins = mm(PB[b][:, 0:N_EXPERTS], x1T[:, k, P * b:P * b + P], rw[:, k, :], k == 0, k == KT - 1)
                ins.then_inc(s["lgt"], 1)
            pe.wait_ge(s["route"], 2)
            mm(PB[2][:, 0:32], before[:, 0:P], msk[:, 0, :], True, False)
            mm(PB[2][:, 32:64], before[:, P:256], msk[:, 0, :], False, False)
            mm(PB[2][:, 32:64], before[:, 0:P], msk[:, 1, :], False, False)
            mm(PB[2][:, 64:96], before[:, P:256], msk[:, 0, :], False, False)
            mm(PB[2][:, 64:96], before[:, P:256], msk[:, 1, :], False, True).then_inc(s["cntp"], 1)
            pe.wait_ge(s["routed"], 2)
            for b in range(TB):
                ins = tr(PB[4][0:N_EXPERTS, P * b:P * b + P], lg[:, b, :], ident)
            ins.then_inc(s["wt_ps"], 1)
            acc = lambda b, h: PB[2 * b + h]

            def gather(h):
                for k in range(4):
                    for b in range(TB):
                        ins = mm(PB[6 + h][:, P * k:P * k + P], x_sb[:, b, P * (4 * h + k):P * (4 * h + k) + P],
                                 oh[:, b, :], k == 0 and b == 0, b == TB - 1)
                ins.then_inc(s["ga"], 1)

            def combine():
                for b in range(TB):
                    for h in range(2):
                        ins = mm(acc(b, h)[:, :], CT[:, b, :], ysb[:, h, :], False, False)
                ins.then_inc(s["comb"], 1)

            def gate_up(e, xs, w, chunk_waits):
                for c in range(GU_CHUNKS):
                    chunk_waits(c)
                    if c == 0:
                        for n in range(4):
                            mm(PB[4 + n // 2][64 * (n % 2):64 * (n % 2) + 64, :], sel[:, e, :],
                               bgu[:, 512 * n:512 * n + 512], True, False)
                    for k in range(2 * c, 2 * c + 2):
                        for n in range(4):
                            ins = mm(PB[4 + n // 2][64 * (n % 2):64 * (n % 2) + 64, :], xs(k),
                                     w[:, k, 512 * n:512 * n + 512], False, k == KT - 1)
                    yield ins

            def down(aT, chunk_waits):
                for c in range(DN_CHUNKS):
                    chunk_waits(c)
                    for k in range(2 * c, 2 * c + 2):
                        for h in range(2):
                            ins = mm(PB[7][64 * h:64 * h + 64, :], aT[:, k % 4, 64 * (k // 4):64 * (k // 4) + 64],
                                     dn_slot[:, k, 512 * h:512 * h + 512], k == 0, k == KT - 1)
                    yield ins

            def act_transposes():
                for c in range(4):
                    ins = tr(PB[6][:, P * c:P * c + P], act_sb[:, P * c:P * c + P], ident)
                return ins

            pe.wait_ge(s["ohs"], 1)
            gather(0)
            gather(1)
            pe.wait_ge(s["ysz"], 1)
            zeros = CTx[:, 0, :].bitcast(BF16)
            for b in range(TB):
                for h in range(2):
                    for q in range(2):
                        mm(acc(b, h)[:, 256 * q:256 * q + 256], zeros[:, 0:P], zeros[:, 0:256], q == 0, False)\
                            .then_inc(s[("xguc", "xdnc")[q]], 1)
            pe.wait_ge(s["bgu_ld"], 16)
            xcount = pe.alloc_register("pe_extra_blocks")
            pe.reg_mov(xcount, 0)

            def extra_gate_up(e):
                pe.reg_add(xcount, xcount, 1)
                xc = pe.snap(xcount, min_val=1, max_val=96)
                pe.wait_ge(s["xoh"], xc)
                for k in range(KT):
                    for b in range(TB):
                        ins = mm(PB[6][:, SLOTS * k:SLOTS * k + SLOTS], x_sb[:, b, P * k:P * k + P], ohx[:, b, :],
                                 k == 0 and b == 0, b == TB - 1)
                ins.then_inc(s["xga"], 1)
                for b in range(TB):
                    ins = tr(PB[7][:, P * b:P * b + P], ohwx[:, b, :], ident)
                ins.then_inc(s["xct"], 1)
                pe.wait_ge(s["xxg"], xc)
                for ins in gate_up(e, lambda k: xgx[:, k, :], gu_slot[e], lambda c: None):
                    ins.then_inc(s["xguc"], 1)
                pe.wait_ge(s["xact"], xc)
                act_transposes().then_inc(s["xat"], 1)
                pe.wait_ge(s["xactT"], xc)
                pe.wait_ge(s["xctd"], xc)

            def extra_down():
                for ins in down(actTx, lambda c: None):
                    ins.then_inc(s["xdnc"], 1)
                xc = pe.snap(xcount, min_val=1, max_val=96)
                pe.wait_ge(s["xyd"], xc)
                for b in range(TB):
                    for h in range(2):
                        mm(acc(b, h)[:, :], CTx[64 * h:64 * h + 64, b, :], yx[64 * h:64 * h + 64, :], False, False)

            with pe.Fori(0, PAIRS) as i:
                for e in range(2):
                    if e == 0:
                        pe.wait_ge(s["xg_ok"], 2 * i + 2)
                        pe.wait_ge(s["oht"], i + 1)

                    def gu_waits(c, e=e):
                        pe.wait_ge(s_gul[e][c], 16 * i + 16)

                    for ins in gate_up(e, lambda k, e=e: xg[:, k, 64 * e:64 * e + 64], gu_slot[e], gu_waits):
                        ins.then_inc(s["guc"], 1)
                    if e == 0:
                        pe.wait_ge(s["ysb_ok"], 2 * i + 1)
                        pe.wait_ge(s["bdn_ld"], 16)
                        combine()
                        tr(PB[6][:, 0:P], ohw[:, 0, :], ident)
                        tr(PB[6][:, P:256], ohw[:, 1, :], ident).then_inc(s["ct"], 1)
                        pe.wait_ge(s["ct_sb"], i + 1)
                    else:
                        pe.wait_ge(s["ohs"], i + 2)
                        pe.wait_ge(s["ysb_ok"], 2 * i + 2)
                        gather(0)
                        gather(1)
                        pe.wait_ge(s["xg_ok"], 2 * i + 4)
                    E1 = 2 * i + (e + 1)
                    pe.wait_ge(s["act"], E1)
                    act_transposes().then_inc(s["at"], 1)
                    pe.wait_ge(s["actT"], E1)

                    n = pe.value_load(nx[0:1, bass.ds(2 * i + e, 1)], min_val=0, max_val=3)
                    with pe.If(n > 0):
                        extra_gate_up(e)
                    pe.nop()

                    def dn_waits(c, e=e):
                        pe.wait_ge(s_dnl[e][c], 16 * i + 16)

                    for c, ins in enumerate(down(actT, dn_waits)):
                        ins.then_inc(s["dn_used"], 1)
                    with pe.If(n > 0):
                        pe.wait_ge(s["ysb_ok"], E1 + 1)
                        extra_down()
                    pe.nop()
                    with pe.If(n > 1):
                        with pe.Fori(1, n):
                            extra_gate_up(e)
                            extra_down()
                    pe.nop()
            pe.wait_ge(s["ysb_ok"], 2 * PAIRS + 1)
            combine()

        @block.vector
        def _(dve):
            link = chain(dve, "v_self")
            ts, tt, stt, cp = dve.tensor_scalar, dve.tensor_tensor, dve.scalar_tensor_tensor, dve.tensor_copy

            dve.wait_ge(s["tables"], 3)
            for r in range(4):
                for g in range(2):
                    stt(alibi[:, 2 * r + g, :], dist, slope(4 * g + r), causal, ALU.mult, ALU.add)
            for b in (0, 2):
                dve.wait_ge(s["xt_ps"], b + 1)
                cp(xT[:, 2 * b:2 * b + 2, :].rearrange("p k t -> p (k t)"), PB[b][:, :]).then_inc(s["xt_sb"], 1)
            dve.wait_ge(s["rows_ps"], 1)
            cp(cols, PB[7][:, 0:N_ROWS]).then_inc(s["kvp_ok"], 1)
            dve.wait_ge(s["kvp_ok"], 1)
            dve.wait_ge(s["bv_ld"], 64)
            dve.wait_ge(s["zer"], 6)
            for n, name in enumerate(outputs):
                if n == 8:
                    dve.wait_ge(s["ev_act"], 2)
                    dve.wait_ge(s["kvp_ok"], 1)
                    for kv in range(2):
                        even = kv2[kv].rearrange("p g (a j e) -> p g a j e", j=8, e=2)[:, :, :, :, 0]
                        for v in range(2):
                            c = 16 * kv + 8 * v
                            ins = [tt(kvp[kv][v].rearrange("p (j a g) -> p g a j", j=8, g=2)[:, g], even[:, g],
                                      posT[:, c:c + 8].unsqueeze(1).broadcast_to([P, 18, 8]), ALU.add)
                                   for g in range(2)][-1]
                        ins.then_inc(s["kvp_ok"], 1)
                if name in by_act:
                    continue
                dve.wait_ge(s["proj"], n + 1)
                ps = PB[n % 8]
                base = name.split(".")[0]
                bias = lambda p0, p1: cols[p0:p1, bcol[base]:bcol[base] + 1]
                if base in toks:
                    c, w, at, _ = toks[base]
                    ins = tt(V[:, int(name[-1]), at:at + w], ps[:, 0:w], bV[:, at:at + w], ALU.add)
                elif base[0] == "q":
                    ins = ts(qn[:, int(base[1]), :], ps[:, 0:256], bias(0, P), SCALE, ALU.add, ALU.mult)
                elif base[0] == "f":
                    ins = ts(fq[:, int(base[2]), :], ps[:, 0:256], bias(0, P), SCALE, ALU.add, ALU.mult)
                else:
                    j = int(base[2])
                    ts(bqz[0:64, j, 0, :], ps[0:64, 0:256], bias(0, 64), SCALE, ALU.add, ALU.mult)
                    ins = ts(bqz[64:128, j, 1, :], ps[64:128, 0:256], bias(64, P), SCALE, ALU.add, ALU.mult)
                ins.then_inc(s["ev_dve"], 1)
            dve.wait_ge(s["ev_dve"], n_dve)
            ts(gs, V[:, :, V_GATE:V_GATE + 24], -80.0, None, ALU.max).then_inc(s["lf_dve"], 1)
            dve.wait_ge(s["hid"], 1)
            link(cp(hx[0:64, :], PB[0][0:64, 0:P]))
            link(tt(h2[0:64, :], hx[0:64, :], hx[0:64, :], ALU.mult))
            link(ts(h2[0:64, :], h2[0:64, :], 0.044715 * GELU_C, GELU_C, ALU.mult, ALU.add))
            tt(hu[0:64, :], h2[0:64, :], hx[0:64, :], ALU.mult).then_inc(s["hid_dve"], 1)
            dve.wait_ge(s["hid_act"], 1)
            stt(hx[0:64, :], hu[0:64, :], 1.0, hx[0:64, :], ALU.add, ALU.mult).then_inc(s["hid_dve"], 1)
            dve.wait_ge(s["lf_act"], 1)
            link(ts(gs, gs, 1.0, None, ALU.add))
            link(dve.reciprocal(gs, gs))
            link(stt(lf, V[:, :, V_F:V_F + 4], 0.0, lt, ALU.min, ALU.subtract))
            for b in range(TB):
                ins = cp(lfb[:, b, :, :], lf[:, b, :].unsqueeze(2).broadcast_to([P, 4, P])).then_inc(s["logf"], 1)
            dve.wait_ge(s["hidt"], 1)
            link(ts(hidT, PB[4][:, 0:64], 0.5, None, ALU.mult))
            for g in range(2):
                ins = cp(hidV.rearrange("p (r g n) -> p r g n", r=4, g=2)[:, :, g, :],
                         hidT[:, 32:64].rearrange("p (n g) -> p g n", g=2)[:, g, :].unsqueeze(1).broadcast_to([P, 4, 16]))
            ins.then_inc(s["hidt_sb"], 1)
            dve.wait_ge(s["clq"], 1)
            link(cp(ncq.rearrange("p b h -> p (b h)"), PB[1][:, 0:8]))
            dve.wait_ge(s["fb_ps"], 1)
            for h in range(4):
                ps = PB[2 + h // 2][:, 256 * (h % 2):256 * (h % 2) + 256]
                stt(fbias[:, h, 0:P], ps[:, 0:P], ncq[:, 0, h:h + 1], causal[:, 0:P], ALU.subtract, ALU.add)
                ins = stt(fbias[:, h, P:384], ps, ncq[:, 1, h:h + 1], causal[:, P:384], ALU.subtract, ALU.add)
            ins.then_inc(s["fb_ok"], 1)
            dve.wait_ge(s["masks"], 4)
            for r in range(4):
                for g in range(2):
                    ins = stt(cb[:, :, 2 * r + g, :], dc, slope(4 * g + r), cm, ALU.mult, ALU.add)
            link(ins)
            dve.wait_ge(s["kcv"], 1)
            kc = PB[5][:, 0:32].rearrange("p (n g) -> p g n", g=2)
            cp(kcz[0:64, 0:16], kc[0:64, 0, :])
            cp(kcz[64:128, 16:32], kc[64:128, 1, :])
            tt(VCZ, PB[6][:, 0:DH].unsqueeze(1).broadcast_to([P, 8, DH]),
               vmask.unsqueeze(2).broadcast_to([P, 8, DH]), ALU.mult).then_inc(s["kcv_sb"], 1)
            dve.wait_ge(s["csc"], 1)
            link(tt(Lc, PB[7][:, 0:256], cb.rearrange("p b h n -> p (b h n)"), ALU.add))
            Lc3 = Lc.rearrange("p (h n) -> p h n", n=16)
            link(dve.tensor_reduce(cmx, Lc3, AX.X, ALU.max))
            tt(Lc3, Lc3, cmx.unsqueeze(2).broadcast_to([P, 16, 16]), ALU.subtract).then_inc(s["cexp_in"], 1)
            dve.wait_ge(s["cexp"], 1)
            link(dve.tensor_reduce(csm, Lc3, AX.X, ALU.add))
            link(dve.reciprocal(csm, csm))
            for b in range(TB):
                c3 = csm[:, 8 * b:8 * b + 8].rearrange("p (r g) -> p r g", g=2)
                ins = stt(c3, c3, avail[:, b:b + 1], gs[:, b, 0:8].rearrange("p (g r) -> p r g", g=2), ALU.mult, ALU.mult)
            link(ins)
            tt(Lc3, Lc3, csm.unsqueeze(2).broadcast_to([P, 16, 16]), ALU.mult).then_inc(s["pc"], 1)

            def ttr(u):
                kind, r = units[u]
                dve.wait_ge(s["sc"], u + 1)
                if u >= 3:
                    dve.wait_ge(s["pts"], 2 * (u - 2))
                l, m = L[u % 3], mx[u % 3]
                for c in range(4):
                    qb, h = c // 2, c % 2
                    w = (P, 256)[qb]
                    src = PB[2 * (u % 2) + qb][:, w * h:w * h + w]
                    tab = (fbias if kind == "fox" else alibi)[:, 2 * r + h, (0, P)[qb]:(P, 384)[qb]]
                    dst = l[:, 256 * qb + w * h:256 * qb + w * h + w]
                    ins = dve.tensor_tensor_reduce(dst, src, tab, 1.0, -3.0e38, ALU.add, ALU.max, m[:, c:c + 1])
                link(ins)
                ts(nmx[u % 3], m, -1.0, None, ALU.mult).then_inc(s["ttr"], 1)

            def scale(u):
                kind, r = units[u]
                dve.wait_ge(s["exp"], u + 1)
                q = rr[u % 3]
                link(dve.reciprocal(q, sm[u % 3]))
                if kind != "fox":
                    n = 8 if kind == "sel" else 16
                    gate = gs[:, :, n:n + 8].rearrange("p b (g r) -> p b g r", g=2)[:, :, :, r]
                    link(tt(q.rearrange("p (b g) -> p b g", b=2), q.rearrange("p (b g) -> p b g", b=2), gate, ALU.mult))
                l = L[u % 3]
                for c, (a, b) in enumerate(((0, 128), (128, 256), (256, 512), (512, 768))):
                    ins = ts(l[:, a:b], l[:, a:b], q[:, c:c + 1], None, ALU.mult)
                ins.then_inc(s["scaled"], 1)

            def ptb(u):
                dve.wait_ge(s["pts"], 2 * u + 2)
                if u >= 2:
                    dve.wait_ge(s["pv"], u - 1)
                cp(PT[u % 2][:, 384:768], PB[5][:, 0:384]).then_inc(s["ptb"], 1)

            def add_square(i):
                kind, r = o_order[i]
                if r > 0:
                    dve.wait_ge(s["oscaled"], i + 1)
                    a = ssq[:, {"nsa": 0, "fox": 1, "sb": 2}[kind], :]
                    tt(a, a, sq, ALU.add).then_inc(s["ssq_acc"], 1)
                    dve.wait_ge(s["ssq_acc"], sum(1 for _, q in o_order[:i + 1] if q > 0))

            for t in range(NU + 3):
                if t < NU:
                    ttr(t)
                if 1 <= t < NU + 1:
                    scale(t - 1)
                if 2 <= t < NU + 2:
                    ptb(t - 2)
                u = t - 3
                if u >= 0:
                    if units[u][0] == "win":
                        add_square(o_index[("nsa", units[u][1])])
                    elif units[u][0] == "fox":
                        add_square(o_index[units[u]])
            for j in range(2):
                dve.wait_ge(s["zs"], j + 1)
                cp(zc[j][:, 512:768], PB[2 * j][:, 0:256])
                cp(zc[j][:, 0:512], PB[2 * j + 1][:, :]).then_inc(s["zcp"], 1)
            ts(y, x_sb, ALPHA, None, ALU.mult).then_inc(s["xa"], 1)
            dve.wait_ge(s["masks"], 6)
            for j in range(2):
                dve.wait_ge(s["sps"], j + 1)
                dve.wait_ge(s["zmk"], j + 1)
                link(stt(sp[j], zc[j], 0.0, sp[j], ALU.max, ALU.add))
                tt(sp[j], sp[j], strict_01, ALU.mult).then_inc(s["spm"], 1)
            for j in range(2):
                dve.wait_ge(s["incl"], j + 1)
                tt(zm[j][:, 512:768], zm[j][:, 512:768], PB[2 * j][:, 0:256], ALU.add)
                tt(zm[j][:, 0:512], zm[j][:, 0:512], PB[2 * j + 1][:, :], ALU.add).then_inc(s["arg"], 1)
            for i in (6, 7):
                add_square(i)
            dve.wait_ge(s["ssqm"], 6)
            dve.wait_ge(s["xa"], 1)
            ts(rms[:, 0:2], PB[0][:, 0:2], 1.0 / 512, RMS_EPS, ALU.mult, ALU.add)
            ts(rms[:, 2:6], PB[0][:, 2:6], 1.0 / 256, RMS_EPS, ALU.mult, ALU.add).then_inc(s["rms_in"], 1)
            dve.wait_ge(s["rms_p"], 1)

            def norm(v, src, b, stats, powered, n, g, bt, dst, last, loaded):
                dve.bn_stats(st[:, 12 * b:12 * b + 6], v[:, b, 0:512])
                link(dve.bn_stats(st[:, 12 * b + 6:12 * b + 12], v[:, b, 512:1024]))
                o = 24 + 4 * b
                link(dve.bn_aggr(st[:, o:o + 2], st[:, 12 * b:12 * b + 12]))
                ts(st[:, o + 1:o + 2], st[:, o + 1:o + 2], LN_EPS, None, ALU.add).then_inc(s[stats], 1)
                dve.wait_ge(s[powered], b + 1)
                link(ts(v[:, b, :], v[:, b, :], st[:, o:o + 1], st[:, o + 2:o + 3], ALU.subtract, ALU.mult))
                dve.wait_ge(s[loaded], n)
                link(tt(v[:, b, :], v[:, b, :], g, ALU.mult))
                tt(dst[:, b, :], v[:, b, :], bt, ALU.add).then_inc(s[last], 1)

            n = 0
            for b in range(TB):
                for h in range(2):
                    for g in range(3):
                        dve.wait_ge(s["op"], n + 1)
                        yh = y[:, b, 512 * h:512 * h + 512]
                        n += 1
                        stt(yh, PB[1 + (n - 1) % 6][:, :], rms[:, 2 * g + b:2 * g + b + 1], yh, ALU.mult, ALU.add)\
                            .then_inc(s["ymix"], 1)
                        dve.wait_ge(s["ymix"], n)
                norm(y, None, b, "lnstat", "lnp", 48, lng, lnb, x_sb, "x1ok", "ln_ld")
            dve.wait_ge(s["x1ok"], 2)
            dve.memset(CTx, 0.0)
            dve.memset(ysb, 0.0).then_inc(s["ysz"], 1)
            dve.memset(posm[:, N_EXPERTS:, :], NOT_ROUTED)
            dve.memset(wts[:, N_EXPERTS:, :], 0.0)
            for b in range(TB):
                dve.wait_ge(s["lgt"], b + 1)
                link(tt(lg[:, b, :], PB[b][:, 0:N_EXPERTS], rb, ALU.add))
                link(dve.max(m8[:, b, :], lg[:, b, :]))
                link(dve.max_index(idx8[:, 8 * b:8 * b + 8], m8[:, b, :], lg[:, b, :]))
                ts(lg[:, b, :], lg[:, b, :], m8[:, b, 0:1], None, ALU.subtract).then_inc(s["ract"], 1)
                link(cp(idx4f[:, 4 * b:4 * b + 4], idx8[:, 8 * b:8 * b + 4]))
                link(tt(oh4[:, b, :, :], iota_s[:, 0:N_EXPERTS].unsqueeze(2).broadcast_to([P, N_EXPERTS, 4]),
                        idx4f[:, 4 * b:4 * b + 4].unsqueeze(1).broadcast_to([P, N_EXPERTS, 4]), ALU.is_equal))
                dve.tensor_reduce(msk[:, b, :], oh4[:, b, :, :], AX.X, ALU.add).then_inc(s["route"], 1)
            dve.wait_ge(s["route"], 2)
            dve.memset(CT, 0.0).then_inc(s["ysz"], 1)
            for b in range(TB):
                dve.wait_ge(s["rsum"], b + 1)
                link(dve.tensor_tensor_reduce(lg[:, b, :], lg[:, b, :], msk[:, b, :], 1.0, 0.0, ALU.mult, ALU.add,
                                              row1[:, b:b + 1]))
                link(dve.reciprocal(row1[:, b:b + 1], row1[:, b:b + 1]))
                link(ts(lg[:, b, :], lg[:, b, :], row1[:, b:b + 1], None, ALU.mult))
                link(cp(wts[:, 0:N_EXPERTS, b], lg[:, b, :]))
            dve.wait_ge(s["cntp"], 1)
            n1, n2 = oh4[:, 0, 0:8, :].rearrange("p e k -> p (e k)"), oh4[:, 0, 8:16, :].rearrange("p e k -> p (e k)")
            link(ts(n1, PB[2][:, 64:96], float(SLOTS), None, ALU.is_gt))
            link(stt(n2, PB[2][:, 64:96], 2.0 * SLOTS, n1, ALU.is_gt, ALU.add))
            link(stt(nx[:, 0:N_EXPERTS], PB[2][:, 64:96], 3.0 * SLOTS, n2, ALU.is_gt, ALU.add))
            for b in range(TB):
                pm = posm[:, 0:N_EXPERTS, b]
                link(stt(pm, PB[2][:, 32 * b:32 * b + 32], -NOT_ROUTED, msk[:, b, :], ALU.add, ALU.mult))
                ts(pm, pm, NOT_ROUTED, None, ALU.add).then_inc(s["routed"], 1)
            dve.wait_ge(s["routed"], 2)

            def one_hots(step):
                ins = None
                for e in range(2):
                    for b in range(TB):
                        pc, wc = curp[:, 2 * e + b:2 * e + b + 1], curw[:, 2 * e + b:2 * e + b + 1]
                        ts(oh[:, b, 64 * e:64 * e + 64], iota_s, pc, None, ALU.is_equal)
                        ins = ts(ohw[:, b, 64 * e:64 * e + 64], iota_s, pc, wc, ALU.is_equal, ALU.mult)
                ins.then_inc(s["ohs"], 1)

            def expert_rows():
                for e in range(2):
                    ins = ts(sel[:, e, :], pidx, ecnt[:, e:e + 1], None, ALU.is_equal)
                ins.then_inc(s["oht"], 1)

            cp(curp, posm[:, 0:2, :].rearrange("p e b -> p (e b)"))
            cp(curw, wts[:, 0:2, :].rearrange("p e b -> p (e b)"))
            dve.memset(ecnt[:, 0:1], 0.0)
            link(dve.memset(ecnt[:, 1:2], 1.0))
            one_hots(0)
            expert_rows()

            def activations(gu_ready, g_ok, clip, upg, sig, done):
                gu_ready()
                ts(gt, PB[4][:, :], LIMIT, None, ALU.min).then_inc(s[g_ok[0]], 1)
                ts(ut, PB[5][:, :], LIMIT, -LIMIT, ALU.min, ALU.max).then_inc(s[clip[0]], 1)
                dve.wait_ge(s[clip[0]], clip[1])
                stt(ut, ut, 1.0, gt, ALU.add, ALU.mult).then_inc(s[upg[0]], 1)
                dve.wait_ge(s[upg[0]], upg[1])
                dve.wait_ge(s[sig[0]], sig[1])
                tt(act_sb, ut, act_sb, ALU.mult).then_inc(s[done], 1)

            xcount = dve.alloc_register("dve_extra_blocks")
            dve.reg_mov(xcount, 0)
            xexperts = dve.alloc_register("dve_experts_with_extra_blocks")
            dve.reg_mov(xexperts, 0)
            with dve.Fori(0, PAIRS) as i:
                for e in range(2):
                    E1 = 2 * i + (e + 1)
                    activations(lambda: dve.wait_ge(s["guc"], E1 * GU_CHUNKS), ("g_ok", 0), ("clip", E1), ("upg", E1),
                                ("sig", E1), "act")
                    if e == 0:
                        cp(curp, posm[:, bass.ds(2 * i + 2, 2), :].rearrange("p e b -> p (e b)"))
                        cp(curw, wts[:, bass.ds(2 * i + 2, 2), :].rearrange("p e b -> p (e b)")).then_inc(s["cur"], 1)
                        dve.wait_ge(s["cur"], i + 1)
                        dve.wait_ge(s["ct"], i + 1)
                        dve.wait_ge(s["ga"], 2 * i + 2)
                        one_hots(1)
                    n = dve.value_load(nx[0:1, bass.ds(2 * i + e, 1)], min_val=0, max_val=3)
                    with dve.If(n > 0):
                        cp(curx, posm[:, bass.ds(2 * i + e, 1), :].rearrange("p e b -> p (e b)"))
                        cp(xw, wts[:, bass.ds(2 * i + e, 1), :].rearrange("p e b -> p (e b)")).then_inc(s["xin"], 1)
                        dve.reg_add(xexperts, xexperts, 1)
                        xe = dve.snap(xexperts, min_val=1, max_val=N_EXPERTS)
                        with dve.Fori(0, n):
                            dve.reg_add(xcount, xcount, 1)
                            xc = dve.snap(xcount, min_val=1, max_val=96)
                            gu_count = dve.snap(xc * 4 + GU_CHUNKS, min_val=1, max_val=4 * 97)
                            dve.wait_ge(s["xin"], xe)
                            ts(curx, curx, -float(SLOTS), None, ALU.add).then_inc(s["xcur"], 1)
                            dve.wait_ge(s["xcur"], xc)
                            for b in range(TB):
                                ts(ohx[:, b, :], iota_s, curx[:, b:b + 1], None, ALU.is_equal)
                                for h in range(2):
                                    ins = ts(ohwx[:, b, 64 * h:64 * h + 64], iota_s, curx[:, b:b + 1], xw[:, b:b + 1],
                                             ALU.is_equal, ALU.mult)
                            ins.then_inc(s["xoh"], 1)
                            activations(lambda: dve.wait_ge(s["xguc"], gu_count), ("xgok", 0), ("xclip", xc),
                                        ("xupg", xc), ("xsig", xc), "xact")
                    dve.nop()
                    if e == 1:
                        ts(ecnt, ecnt, 2.0, None, ALU.add).then_inc(s["cse"], 1)
                        dve.wait_ge(s["cse"], i + 1)
                        expert_rows()
            dve.wait_ge(s["comb"], PAIRS + 1)
            for b in range(TB):
                for h in range(2):
                    ins = stt(yf[:, b, 512 * h:512 * h + 512], x_sb[:, b, 512 * h:512 * h + 512], ALPHA,
                              PB[2 * b + h][:, :], ALU.mult, ALU.add)
                link(ins)
                norm(yf, None, b, "fin", "flnp", 32, fg, fb, yf, "fout", "ln2_ld")

    return nc


_INS = ['x', 'w_in', 'b_in', 'cmp_pos_k', 'cmp_pos_v', 'cmp_w1_k', 'cmp_w2_k', 'cmp_w1_v', 'cmp_w2_v', 'g_out', 'w_out',
        'ln1_g', 'ln1_b', 'router_w', 'router_b', 'w_gate_up', 'b_gate_up', 'w_down', 'b_down', 'ln2_g', 'ln2_b']
_OUTS = [((1, 256, 1024), 'float32')]


def kernel(**inputs):
    import numpy as _np
    import concourse.bacc as _bacc
    from concourse import mybir as _mybir
    from concourse.bass_utils import run_bass_kernel_spmd as _run

    nc = _bacc.Bacc("TRN2", target_bir_lowering=False, num_devices=1)
    arrays, args = {}, []
    for name in _INS:
        a = _np.ascontiguousarray(inputs[name])
        arrays[f"in_{name}_dram"] = a
        args.append(nc.dram_tensor(f"in_{name}_dram", a.shape, _mybir.dt.from_np(a.dtype), kind="ExternalInput").ap())
    for i, (shape, dtype) in enumerate(_OUTS):
        dt = _mybir.dt.from_np(_np.dtype(dtype))
        args.append(nc.dram_tensor(f"out_{i}_dram", shape, dt, kind="ExternalOutput").ap())
    hybrid_layer(nc, *args)
    r = _run(nc, [arrays], core_ids=[0])
    return r.results[0]["out_0_dram"]
```

```python
from contextlib import ExitStack

import concourse.bass as bass
from concourse import mybir

ALU = mybir.AluOpType
ACT = mybir.ActivationFunctionType
AX = mybir.AxisListType
F32 = mybir.dt.float32
BF16 = mybir.dt.bfloat16
U32 = mybir.dt.uint32
I32 = mybir.dt.int32

P = 128
TOKENS = 256
TB = TOKENS // P
D = 1024
KT = D // P
DH = 64
CMP_LEN, CMP_STRIDE, CMP_BLOCKS = 32, 16, 16
N_EXPERTS = 32
TOP_K = 4
PAIRS = N_EXPERTS // 2
SLOTS = 64
XSLOTS = 32
MAX_EXTRA = (TOKENS - SLOTS) // XSLOTS
EXPERTS_PADDED = N_EXPERTS + 2
GU_CHUNKS = 4
DN_CHUNKS = 4
ALPHA = 2.0 ** 0.25
SCALE = DH ** -0.5
LN_EPS, RMS_EPS = 1e-5, 1e-6
LIMIT, SWIGLU_ALPHA = 7.0, 1.702
MASKED = -1e30
NOT_ROUTED = -4096.0
N_ROWS, G_OUT_COL = 57, 49
GELU_C = 0.7978845608028654

C_Q, C_KC, C_VC, C_KS, C_VS, C_KW, C_VW, C_GATE = 0, 512, 640, 768, 896, 1024, 1152, 1280
C_FQ, C_FK, C_FV, C_FF, C_BQ, C_BK, C_BV, D_IN = 1304, 1560, 1816, 2072, 2076, 2332, 2588, 2844
V_SEL, V_WIN, V_GATE, V_FOX, V_F, V_SB, V_COLS = 0, 128, 256, 280, 536, 540, 796


W_IN_GROUPS = [(C_KC, C_KS), (C_KS, C_FQ), (0, C_KC), (C_FQ, C_BQ), (C_BQ, D_IN)]


def slope(head):
    return 2.0 ** (-8.0 * (head + 1) / 8)


def hybrid_layer(nc, x, w_in, b_in, pos_k, pos_v, w1_k, w2_k, w1_v, w2_v, g_out, w_out, ln1_g, ln1_b,
                 router_w, router_b, w_gu, b_gu, w_dn, b_dn, ln2_g, ln2_b, out):
    with ExitStack() as ctx:
        def sb(name, cols, dt=F32):
            return ctx.enter_context(nc.sbuf_tensor(name, [P, cols], dt))

        def sem(name):
            return ctx.enter_context(nc.semaphore(name))

        GU = KT * 2 * D
        WB = sb("WB", 2 * GU + KT * D)
        reg_b, reg_a, reg_dn = WB[:, 0:GU], WB[:, GU:2 * GU], WB[:, 2 * GU:2 * GU + KT * D]
        gu_slot = [reg_a.rearrange("p (k n) -> p k n", k=KT), reg_b.rearrange("p (k n) -> p k n", k=KT)]
        dn_slot = reg_dn.rearrange("p (k n) -> p k n", k=KT)
        w_in_sb = WB[:, GU:GU + KT * D_IN].rearrange("p (k n) -> p k n", k=KT)
        wo_sb = dn_slot

        def carver(region):
            at = [0]

            def take(cols, **shape):
                a = region[:, at[0]:at[0] + cols]
                at[0] += cols
                if shape:
                    names = " ".join(shape)
                    a = a.rearrange(f"p ({names}) -> p {names}", **shape)
                return a
            return take

        X = sb("X", TB * D)
        x_sb = X[:, :].rearrange("p (b d) -> p b d", b=TB)
        S1 = sb("S1", KT * TOKENS)
        oT = S1[:, :].rearrange("p (k t) -> p k t", k=KT)
        bgu = S1[:, :]
        S2 = sb("S2", 6656)
        take = carver(S2[:, :])
        x1T = take(KT * TOKENS, k=KT, t=TOKENS)
        xT = x1T
        y = take(TB * D, b=TB, d=D)
        lng = take(D)
        lnb = take(D)
        rw = take(KT * N_EXPERTS, k=KT, e=N_EXPERTS)
        take = carver(S2[:, KT * TOKENS:])
        alibi = take(8 * 384, h=8, k=384)
        causal = take(384)
        dist = take(384)
        take = carver(S2[:, :])
        xg = take(KT * 2 * SLOTS, k=KT, s=2 * SLOTS)
        gt = take(512)
        ut = take(512)
        act_sb = take(512)
        actT = take(512, c=4, s=P)
        ysb = take(1024, n=2, d=512)
        actTx = take(256, c=4, s=2 * XSLOTS)
        act_x = yx = take(512)
        xgx = yx[:, 0:KT * XSLOTS].rearrange("p (k s) -> p k s", k=KT)
        CTx = take(TB * P, b=TB, t=P)
        ohwx = take(TB * P, b=TB, s=P)
        ohx = take(TB * XSLOTS, b=TB, s=XSLOTS)
        ohw = take(TB * P, b=TB, s=P)
        CT = take(TB * P, b=TB, t=P)
        oh = take(TB * P, b=TB, s=P)
        sel = take(2 * SLOTS, e=2, s=SLOTS)
        yf = S2[:, 0:TB * D].rearrange("p (b d) -> p b d", b=TB)
        fg, fb = reg_a[:, 0:D], reg_a[:, D:2 * D]

        K = sb("K", 1170)
        take = carver(K[:, :])
        ident = take(P)
        iota_s = take(SLOTS)
        pidx = take(SLOTS)
        posm = take(EXPERTS_PADDED * TB, e=EXPERTS_PADDED, b=TB)
        wts = take(EXPERTS_PADDED * TB, e=EXPERTS_PADDED, b=TB)
        lg = take(TB * N_EXPERTS, b=TB, e=N_EXPERTS)
        msk = take(TB * N_EXPERTS, b=TB, e=N_EXPERTS)
        m8 = take(TB * 8, b=TB, e=8)
        oh4 = take(TB * 4 * N_EXPERTS, b=TB, e=N_EXPERTS, k=4)
        st = take(TB * 12 + 4 * TB)
        rb = take(N_EXPERTS)
        rms = take(8)
        half = take(8)
        curp = take(4)
        curw = take(4)
        curx = take(2)
        xw = take(2)
        ecnt = take(2)
        row1 = take(16)
        before = take(2 * P)
        idx8 = sb("idx8", TB * 8, U32)
        nx = sb("nx", EXPERTS_PADDED, I32)
        idx4f = sb("idx4f", TB * 4)

        take = carver(reg_b)
        QUARTER = GU // GU_CHUNKS
        qn = take(4 * TOKENS, r=4, t=TOKENS)
        kzs = take(512, g=2, t=TOKENS)
        kzw = take(512, g=2, t=TOKENS)
        bV = take(V_COLS)
        kv2_at = 4 * TOKENS + 2 * 512 + V_COLS
        kv2 = [take(576, g=2, t=288) for _ in range(2)]
        take = carver(reg_b[:, QUARTER:])
        w1 = [take(2048, j=16, n=P) for _ in range(2)]
        kvp = [[take(288) for _ in range(2)] for _ in range(2)]
        fq = take(512, j=2, t=TOKENS)
        fkz = take(1024, j=2, h=2, t=TOKENS)
        bk = take(512, j=2, t=TOKENS)
        bqz = take(1024, j=2, h=2, t=TOKENS)
        V = take(TB * V_COLS, b=TB, c=V_COLS)
        le_ones = take(256)
        neg_ge = take(P)
        take_b = take
        take = carver(reg_b[:, QUARTER:QUARTER + 4096])
        L = [take(768) for _ in range(3)]
        PT = [take(768) for _ in range(2)]
        Lc = take(256)
        take = carver(reg_b[:, QUARTER + 4096:QUARTER + 4096 + 4 * 288])
        sq = take(256)
        ssq = take(3 * 256, g=3, t=TOKENS)
        hidT = take(64)
        take = carver(reg_b[:, kv2_at:QUARTER])
        VCZ = take(512, h=8, d=DH)
        PcT = take(256)
        cb = take(256, b=TB, h=8, n=16)
        hidV = take(P)
        take = carver(S2[:, 5888:])
        hx = take(P)
        h2 = take(P)
        hu = take(P)
        kcz = take(32)
        dc = take(32, b=TB, n=16)
        vmask = take(8)
        cm = take(32, b=TB, n=16)
        take = carver(reg_a[:, 0:GU // 2])
        fbias = take(4 * 384, h=4, k=384)
        strict_add = take(768)
        strict_01 = take(768)
        zc = [take(768) for _ in range(2)]
        sp = [take(768) for _ in range(2)]
        zm = [take(768) for _ in range(2)]
        lfb = S2[:, 0:TB * 4 * P].rearrange("p (b h q) -> p b h q", b=TB, h=4)
        take = take_b
        w2sb = take(2 * DH)
        rows = take(P)
        cols = take(N_ROWS)
        posT = cols[:, 0:32]
        mx = [take(4) for _ in range(3)]
        nmx = [take(4) for _ in range(3)]
        sm = [take(4) for _ in range(3)]
        rr = [take(4) for _ in range(3)]
        gs = take(TB * 24, b=TB, c=24)
        avail = take(2)
        lf = take(TB * 4, b=TB, h=4)
        lt = take(TB * 4, b=TB, h=4)
        ncq = take(TB * 4, b=TB, h=4)
        cmx = take(16)
        csm = take(16)
        ones1 = take(1)
        PB = [ctx.enter_context(nc.psum_tensor(f"PB{i}", [P, 512], F32)) for i in range(8)]

        names = """x_in smalls rows_ld rows_ps bv_ld w1ld wo_ld ln_ld ln2_ld bdn_ld bgu_ld cst zer xt_ps xt_sb proj ev_dve ev_act
        kvp_ok g_in g_exp hid hid_dve hid_act hidt hidt_sb kcv kcv_sb csc cexp_in cexp pc pct pct_sb logf lf_dve lf_act
        clq clq_sb fb_ps fb_ok tables masks sc ttr exp scaled pts pta ptb pv sqs oscaled ssq_acc
        zs zcp zabs sps zmk spm incl arg aexp ssqm rms_in rms_p rms_ok op ymix lnstat lnp lnok x1ok x1t x1tsb lgt
        route ract rsum cntp routed xin ysz ysb_ok clip upg cur cse xclip xupg xcur wt_ps wt_sb accinit xa
        ohs oht ga xg_ok guc g_ok sig act at actT dn_used ct ct_sb comb xsec
        xoh xga xxg xct xctd xgu gu xguc xdnc xgok xsig xact xat xactT xyd fin flnp fout outd v_self a_self p_self""".split()
        s = {n: sem("s_" + n) for n in names}
        s_win = [sem(f"s_win{i}") for i in range(5)]
        s_gul = [[sem(f"s_gul{e}{c}") for c in range(GU_CHUNKS)] for e in range(2)]
        s_dnl = [[sem(f"s_dnl{e}{c}") for c in range(DN_CHUNKS)] for e in range(2)]
        block = ctx.enter_context(nc.Block())

        feat = [("kc", C_KC, 0), ("vc", C_VC, 0), ("ks", C_KS, 1), ("kw", C_KW, 1),
                ("q0", 0, 2), ("q1", 1, 2), ("q2", 2, 2), ("q3", 3, 2),
                ("fq0", C_FQ, 3), ("fq1", C_FQ + P, 3), ("fk0", C_FK, 3), ("fk1", C_FK + P, 3),
                ("bq0", C_BQ, 4), ("bq1", C_BQ + P, 4), ("bk0", C_BK, 4), ("bk1", C_BK + P, 4)]
        toks = {"vs": (C_VS, 128, V_SEL, 1), "vw": (C_VW, 152, V_WIN, 1), "vf": (C_FV, 260, V_FOX, 3),
                "vb": (C_BV, 256, V_SB, 4)}
        early = ["kc", "vc", "ks", "kw", "vw.0", "vw.1", "q0", "q1", "q2", "q3", "vs.0", "vs.1"]
        late = ["fq0", "fq1", "fk0", "fk1", "vf.0", "vf.1", "bq0", "bq1", "bk0", "bk1", "vb.0", "vb.1"]
        outputs = early + late
        fdict = {f[0]: f for f in feat}
        bcol = {"kc": 32, "vc": 33, "ks": 34, "kw": 36, "q0": 37, "q1": 38, "q2": 39, "q3": 40, "fq0": 41, "fq1": 42,
                "fk0": 43, "fk1": 44, "bq0": 45, "bq1": 46, "bk0": 47, "bk1": 48}
        by_act = {"kc", "vc", "ks", "kw", "fk0", "fk1", "bk0", "bk1"}
        ready, n_dve, n_act = {}, 0, 0
        for o in outputs:
            if o in by_act:
                n_act += 1
                ready[o] = ("ev_act", n_act)
            else:
                n_dve += 1
                ready[o] = ("ev_dve", n_dve)
        units = [(b, r) for r in range(4) for b in ("sel", "win")] + [("fox", 0), ("fox", 1)]
        NU = len(units)
        NSA = 8
        op_order = [(0, b, h) for b in range(TB) for h in range(2)] + \
                   [(g, b, h) for b in range(TB) for g in (1, 2) for h in range(2)]
        op_bank = [1 + n % 5 for n in range(len(op_order))]
        x1t_bank = lambda b, h: (6, 4)[b] + h
        op_k = ((0, 1, 2, 3), (4, 5), (6, 7))
        o_order = [("nsa", r) for r in range(4)] + [("fox", 0), ("fox", 1), ("sb", 0), ("sb", 1)]
        o_index = {k: i for i, k in enumerate(o_order)}

        def need(eng, what):
            n, v = ready[what]
            eng.wait_ge(s[n], v)

        def chain(eng, name):
            n = [0]

            def link(ins):
                n[0] += 1
                ins.then_inc(s[name], 1)
                eng.wait_ge(s[name], n[0])
            return link

        @block.sync
        def _(sp_):
            sp = sp_
            sp.dma_start(x_sb, x[0].rearrange("(b p) d -> p b d", p=P)).then_inc(s["x_in"], 16)
            w_v = w_in[0].rearrange("(k p) n -> p k n", p=P)
            for dst, src in ((rows[0:16, :], pos_k[0].rearrange("(j a) d -> j (a d)", a=2)),
                             (rows[16:32, :], pos_v[0].rearrange("(j a) d -> j (a d)", a=2)),
                             (rows[32:37, :], b_in[0, C_KC:C_KC + 5 * P].rearrange("(r n) -> r n", n=P)),
                             (rows[37:41, :].rearrange("r (g d) -> r g d", g=2),
                              b_in[0, 0:C_KC].rearrange("(g r d) -> r g d", g=2, r=4)),
                             (rows[41:45, :], b_in[0, C_FQ:C_FQ + 4 * P].rearrange("(r n) -> r n", n=P)),
                             (rows[45:49, :], b_in[0, C_BQ:C_BQ + 4 * P].rearrange("(r n) -> r n", n=P)),
                             (rows[49:53, :].rearrange("r (g d) -> r g d", g=2),
                              g_out[0, 0:512].rearrange("(g r d) -> r g d", g=2, r=4)),
                             (rows[53:57, :], g_out[0, 512:D].rearrange("(r n) -> r n", n=P))):
                sp.dma_start(dst, src).then_inc(s["rows_ld"], 16)
            for i, (a, b) in enumerate(W_IN_GROUPS):
                sp.dma_start(w_in_sb[:, :, a:b], w_v[:, :, a:b]).then_inc(s_win[i], 16)
                if i == 2:
                    for kv, w in enumerate((w1_k, w1_v)):
                        sp.dma_start(w1[kv], w[0].rearrange("(j p) n -> p j n", p=P)).then_inc(s["w1ld"], 16)
                if i == 0:
                    for c, n, at, _ in toks.values():
                        sp.dma_start(bV[:, at:at + n], b_in[0:1, c:c + n].broadcast_to([P, n])).then_inc(s["bv_ld"], 16)
            sp.wait_ge(s["proj"], len(outputs))
            for g in range(2):
                sp.dma_start(wo_sb[64 * g:64 * g + 64, 0:4, :],
                             w_out[0, 256 * g:256 * g + 256, :].rearrange("(r p) n -> p r n", p=DH)).then_inc(s["wo_ld"], 16)
            sp.dma_start(wo_sb[:, 4:8, :], w_out[0, 512:1024, :].rearrange("(r p) n -> p r n", p=P)).then_inc(s["wo_ld"], 16)
            gu_v = w_gu[0].rearrange("e (k p) n -> e p k n", p=P)
            dn_v = w_dn[0].rearrange("e (k p) n -> e p k n", p=P)

            def load_gu(i, par, c):
                kk = KT // GU_CHUNKS
                src = gu_v[2 * i + par] if isinstance(i, int) else gu_v[bass.ds(2 * i + par, 1)].rearrange("e p k n -> (e p) k n")
                sp.dma_start(gu_slot[par][:, kk * c:kk * c + kk, :], src[:, kk * c:kk * c + kk, :]).then_inc(s_gul[par][c], 16)

            def load_dn(i, par, c):
                kk = KT // DN_CHUNKS
                src = dn_v[2 * i + par] if isinstance(i, int) else dn_v[bass.ds(2 * i + par, 1)].rearrange("e p k n -> (e p) k n")
                sp.dma_start(dn_slot[:, kk * c:kk * c + kk, :], src[:, kk * c:kk * c + kk, :]).then_inc(s_dnl[par][c], 16)

            def count_extra_blocks(e):
                n = sp.value_load(nx[0:1, e:e + 1] if isinstance(e, int) else nx[0:1, bass.ds(e, 1)], min_val=0, max_val=MAX_EXTRA)
                sp.reg_add(xcount, xcount, n)

            def use_by_extra_blocks(c):
                return sp.snap(sp.snap(xcount, min_val=0, max_val=96) * 4 + (c + 1), min_val=1, max_val=4 * 97)

            sp.wait_ge(s["fb_ok"], 1)
            sp.wait_ge(s["ttr"], NSA)
            for t, src in ((lng, ln1_g), (lnb, ln1_b)):
                sp.dma_start(t, src[0:1, :].broadcast_to([P, D])).then_inc(s["ln_ld"], 16)
            sp.dma_start(rw, router_w[0].rearrange("(k p) e -> p k e", p=P)).then_inc(s["ln_ld"], 16)
            for c in (2, 3):
                load_gu(0, 0, c)
            sp.wait_ge(s["pv"], NSA)
            load_gu(0, 1, 0)
            sp.wait_ge(s["pv"], NU + 2)
            sp.wait_ge(s["oscaled"], 8)
            sp.wait_ge(s["ssqm"], 6)

            xcount = sp.alloc_register("sp_extra_blocks")
            sp.reg_mov(xcount, 0)
            for c in (0, 1):
                load_gu(0, 0, c)
            for c in range(1, GU_CHUNKS):
                load_gu(0, 1, c)
            sp.wait_ge(s["op"], 12)
            for c in range(DN_CHUNKS):
                load_dn(0, 0, c)
            sp.wait_ge(s["routed"], 1)
            with sp.Fori(0, PAIRS - 1) as i:
                for par in range(2):
                    count_extra_blocks(2 * i + par)
                    for c in range(GU_CHUNKS):
                        xc = use_by_extra_blocks(c)
                        sp.wait_ge(s["guc"], i * (2 * GU_CHUNKS) + (par * GU_CHUNKS + c + 1))
                        sp.wait_ge(s["xguc"], xc)
                        load_gu(i + 1, par, c)
                    for c in range(DN_CHUNKS):
                        xc = use_by_extra_blocks(c)
                        sp.wait_ge(s["dn_used"], i * (2 * DN_CHUNKS) + (par * DN_CHUNKS + c + 1))
                        sp.wait_ge(s["xdnc"], xc)
                        load_dn(i + par, 1 - par, c)
            count_extra_blocks(N_EXPERTS - 2)
            for c in range(DN_CHUNKS):
                xc = use_by_extra_blocks(c)
                sp.wait_ge(s["dn_used"], (N_EXPERTS - 2) * DN_CHUNKS + c + 1)
                sp.wait_ge(s["xdnc"], xc)
                load_dn(PAIRS - 1, 1, c)
            sp.wait_ge(s["guc"], N_EXPERTS * GU_CHUNKS)
            for t, src in ((fg, ln2_g), (fb, ln2_b)):
                sp.dma_start(t, src[0:1, :].broadcast_to([P, D])).then_inc(s["ln2_ld"], 16)
            for b in range(TB):
                sp.wait_ge(s["fout"], b + 1)
                sp.dma_start(out[0, P * b:P * b + P, :], yf[:, b, :]).then_inc(s["outd"], 16)
            sp.wait_ge(s["outd"], 16 * TB)

        @block.gpsimd
        def _(pool):
            link = chain(pool, "p_self")
            sel_op = pool.affine_select
            link(pool.memset(ident, 0.0))
            sel_op(out=ident, in_=ident, compare_op=ALU.not_equal, fill=1.0, base=0, pattern=[[-1, P]],
                   channel_multiplier=1).then_inc(s["cst"], 1)
            link(pool.memset(causal, 0.0))
            link(sel_op(out=causal[:, 0:P], in_=causal[:, 0:P], compare_op=ALU.is_ge, fill=MASKED, base=0,
                        pattern=[[-1, P]], channel_multiplier=1))
            sel_op(out=causal[:, P:384], in_=causal[:, P:384], compare_op=ALU.is_ge, fill=MASKED, base=P,
                   pattern=[[-1, 256]], channel_multiplier=1).then_inc(s["tables"], 1)
            pool.iota(dist[:, 0:P], [[1, P]], base=0, channel_multiplier=-1,
                      allow_small_or_imprecise_dtypes=True).then_inc(s["tables"], 1)
            pool.iota(dist[:, P:384], [[1, 256]], base=-P, channel_multiplier=-1,
                      allow_small_or_imprecise_dtypes=True).then_inc(s["tables"], 1)
            for t in (kzs, kzw, fkz, bqz, kv2[0], kv2[1]):
                pool.memset(t, 0.0).then_inc(s["zer"], 1)
            link(pool.memset(le_ones, -1.0))
            sel_op(out=le_ones[:, 0:P], in_=le_ones[:, 0:P], compare_op=ALU.is_ge, fill=0.0, base=0,
                   pattern=[[1, P]], channel_multiplier=-1).then_inc(s["tables"], 1)
            link(pool.memset(neg_ge, -1.0))
            sel_op(out=neg_ge, in_=neg_ge, compare_op=ALU.is_ge, fill=0.0, base=0,
                   pattern=[[-1, P]], channel_multiplier=1).then_inc(s["tables"], 1)
            pool.iota(iota_s, [[1, SLOTS]], base=0, channel_multiplier=0,
                      allow_small_or_imprecise_dtypes=True).then_inc(s["tables"], 1)
            pool.iota(pidx, [[0, SLOTS]], base=0, channel_multiplier=1,
                      allow_small_or_imprecise_dtypes=True).then_inc(s["tables"], 1)
            link(pool.memset(avail, 1.0))
            sel_op(out=avail[:, 0:1], in_=avail[:, 0:1], compare_op=ALU.is_ge, fill=0.0, base=-(CMP_LEN - 1),
                   pattern=[[0, 1]], channel_multiplier=1).then_inc(s["tables"], 1)
            pool.memset(half, -0.5).then_inc(s["tables"], 1)
            pool.memset(ones1, 1.0).then_inc(s["tables"], 1)
            link(pool.memset(before, 1.0))
            sel_op(out=before[:, 0:P], in_=before[:, 0:P], compare_op=ALU.is_ge, fill=0.0, base=-1,
                   pattern=[[1, P]], channel_multiplier=-1).then_inc(s["tables"], 1)
            pool.iota(dc, [[-P, TB], [CMP_STRIDE, 16]], base=CMP_LEN - 1, channel_multiplier=-1,
                      allow_small_or_imprecise_dtypes=True).then_inc(s["masks"], 1)
            link(pool.memset(vmask, 1.0))
            link(sel_op(out=vmask, in_=vmask, compare_op=ALU.is_ge, fill=0.0, base=0, pattern=[[-16, 8]],
                        channel_multiplier=1))
            sel_op(out=vmask, in_=vmask, compare_op=ALU.is_ge, fill=0.0, base=15, pattern=[[16, 8]],
                   channel_multiplier=-1).then_inc(s["masks"], 1)
            pool.memset(kcz, 0.0).then_inc(s["masks"], 1)
            link(pool.memset(cm, 0.0))
            sel_op(out=cm, in_=cm, compare_op=ALU.is_ge, fill=MASKED, base=-(CMP_LEN - 1),
                   pattern=[[P, TB], [-CMP_STRIDE, 16]], channel_multiplier=1).then_inc(s["masks"], 1)
            pool.wait_ge(s["proj"], len(outputs))
            for t, base, fill in ((strict_add, 0.0, MASKED), (strict_01, 1.0, 0.0)):
                link(pool.memset(t, base))
                link(sel_op(out=t[:, 0:512], in_=t[:, 0:512], compare_op=ALU.is_ge, fill=fill, base=-1,
                            pattern=[[0, 2], [1, 256]], channel_multiplier=-1))
                sel_op(out=t[:, 512:768], in_=t[:, 512:768], compare_op=ALU.is_ge, fill=fill, base=-1,
                       pattern=[[0, 2], [1, P]], channel_multiplier=-1).then_inc(s["masks"], 1)
            pool.wait_ge(s["ttr"], NSA)
            pool.tensor_scalar(y, x_sb, ALPHA, None, ALU.mult).then_inc(s["xa"], 1)
            for j in range(2):
                pool.wait_ge(s["zcp"], j + 1)
                if j == 0:
                    pool.wait_ge(s["masks"], 6)
                pool.tensor_tensor(zm[j], zc[j], strict_add, ALU.add).then_inc(s["zmk"], 1)
            for g in range(3):
                pool.wait_ge(s["rms_in"], g + 1)
                pool.tensor_tensor(rms[:, 2 * g:2 * g + 2], rms[:, 2 * g:2 * g + 2], half[:, 0:2], ALU.pow)\
                    .then_inc(s["rms_p"], 1)
            for b in range(TB):
                pool.wait_ge(s["lnstat"], b + 1)
                pool.tensor_tensor(st[:, 24 + 4 * b + 2:24 + 4 * b + 3], st[:, 24 + 4 * b + 1:24 + 4 * b + 2],
                                   half[:, 0:1], ALU.pow).then_inc(s["lnp"], 1)
            for b in range(TB):
                pool.wait_ge(s["fin"], b + 1)
                pool.tensor_tensor(st[:, 24 + 4 * b + 2:24 + 4 * b + 3], st[:, 24 + 4 * b + 1:24 + 4 * b + 2],
                                   half[:, 0:1], ALU.pow).then_inc(s["flnp"], 1)

        @block.scalar
        def _(act):
            link = chain(act, "a_self")

            for dst, src in ((w2sb[:, 0:DH], w2_k[0]), (w2sb[:, DH:2 * DH], w2_v[0]),
                             (rb, router_b[0:1, :].broadcast_to([P, N_EXPERTS]))):
                act.dma_start(dst, src).then_inc(s["smalls"], 16)

            for b in (1, 3):
                act.wait_ge(s["xt_ps"], b + 1)
                act.activation(xT[:, 2 * b:2 * b + 2, :].rearrange("p k t -> p (k t)"), PB[b][:, :], ACT.Copy)\
                   .then_inc(s["xt_sb"], 1)
            act.wait_ge(s["kvp_ok"], 1)
            act.wait_ge(s["zer"], 6)

            def bias_copy(dst, src, name, p0, p1):
                return act.activation(dst, src, ACT.Identity, bias=cols[p0:p1, bcol[name]:bcol[name] + 1])

            def evict(n):
                name = outputs[n]
                if name not in by_act:
                    return
                act.wait_ge(s["proj"], n + 1)
                ps = PB[n % 2]
                if name in ("kc", "vc"):
                    d = kv2[0 if name == "kc" else 1]
                    bias_copy(d[0:64, 0, 0:256], ps[0:64, 0:256], name, 0, 64)
                    bias_copy(d[64:128, 1, 0:255], ps[64:128, 1:256], name, 64, 128)
                    bias_copy(d[64:128, 0, 0:255], ps[0:64, 1:256], name, 0, 64)
                    bias_copy(d[0:64, 1, 0:256], ps[64:128, 0:256], name, 64, 128).then_inc(s["ev_act"], 1)
                elif name in ("bk0", "bk1"):
                    bias_copy(bk[:, int(name[-1]), :], ps[:, 0:256], name, 0, 128).then_inc(s["ev_act"], 1)
                else:
                    d = {"ks": kzs, "kw": kzw, "fk0": fkz[:, 0], "fk1": fkz[:, 1]}[name]
                    bias_copy(d[0:64, 0, :], ps[0:64, 0:256], name, 0, 64)
                    bias_copy(d[64:128, 1, :], ps[64:128, 0:256], name, 64, 128).then_inc(s["ev_act"], 1)

            for n in range(len(early)):
                evict(n)
            act.wait_ge(s["hid_dve"], 1)
            act.activation(hu[0:64, :], hu[0:64, :], ACT.Tanh).then_inc(s["hid_act"], 1)
            act.wait_ge(s["g_in"], 1)
            act.activation(gs, gs, ACT.Exp, scale=-1.0).then_inc(s["g_exp"], 1)
            act.wait_ge(s["cexp_in"], 1)
            act.activation(Lc, Lc, ACT.Exp).then_inc(s["cexp"], 1)

            def exps(u):
                act.wait_ge(s["ttr"], u + 1)
                l = L[u % 3]
                for c, (a, b) in enumerate(((0, 128), (128, 256), (256, 512), (512, 768))):
                    ins = act.activation(l[:, a:b], l[:, a:b], ACT.Exp, bias=nmx[u % 3][:, c:c + 1],
                                         accum_out=sm[u % 3][:, c:c + 1])
                ins.then_inc(s["exp"], 1)

            def pta(u):
                act.wait_ge(s["pts"], 2 * u + 1)
                if u >= 2:
                    act.wait_ge(s["pv"], u - 1)
                act.activation(PT[u % 2][:, 0:384], PB[4][:, 0:384], ACT.Copy).then_inc(s["pta"], 1)

            def squares(i):
                kind, r = o_order[i]
                last = {"nsa": 2 * r + 2, "fox": 9 + r, "sb": NU + 1 + r}[kind]
                act.wait_ge(s["pv"], last)
                ps = PB[6 + i % 2][:, 0:256]
                g = {"nsa": 0, "fox": 1, "sb": 2}[kind]
                first = r == 0
                if not first:
                    act.wait_ge(s["ssq_acc"], sum(1 for k, rr_ in o_order[:i] if rr_ > 0))
                link(act.activation(ssq[:, g, :] if first else sq, ps, ACT.Square))
                act.activation(oT[:, i, :], ps, ACT.Copy, scale=cols[:, G_OUT_COL + i:G_OUT_COL + i + 1]).then_inc(s["oscaled"], 1)

            for t in range(NSA + 3):
                if t < NSA:
                    exps(t)
                if t == 0:
                    act.wait_ge(s["pct"], 1)
                    act.activation(PcT, PB[5][:, 0:256], ACT.Copy).then_inc(s["pct_sb"], 1)
                if 2 <= t < NSA + 2:
                    pta(t - 2)
                if t >= 3 and units[t - 3][0] == "win":
                    squares(o_index[("nsa", units[t - 3][1])])
                evict(len(early) + t)
                if t == 6:
                    act.wait_ge(s["ev_dve"], ready["vf.1"][1])
                    link(act.activation(lt, V[:, :, V_F:V_F + 4], ACT.Abs))
                    link(act.activation(lt, lt, ACT.Exp, scale=-1.0))
                    act.activation(lt, lt, ACT.Ln, bias=1.0).then_inc(s["lf_act"], 1)
            for j in range(2):
                act.wait_ge(s["zcp"], j + 1)
                link(act.activation(sp[j], zc[j], ACT.Abs))
                link(act.activation(sp[j], sp[j], ACT.Exp, scale=-1.0))
                if j == 0:
                    exps(NSA)
            for j in range(2):
                act.activation(sp[j], sp[j], ACT.Ln, bias=1.0).then_inc(s["sps"], 1)
            exps(NSA + 1)
            pta(NSA)
            for j in range(2):
                act.wait_ge(s["arg"], j + 1)
                act.activation(zm[j], zm[j], ACT.Exp).then_inc(s["aexp"], 1)
                if j == 0:
                    squares(4)
                    pta(NSA + 1)
            for i in (5, 6, 7):
                squares(i)

            act.wait_ge(s["op"], 12)
            act.dma_start(bgu[0:N_EXPERTS, :], b_gu[0]).then_inc(s["bgu_ld"], 16)
            for b in range(TB):
                for h in range(2):
                    act.wait_ge(s["x1t"], 2 * b + h + 1)
                    act.activation(x1T[:, 4 * h:4 * h + 4, P * b:P * b + P],
                                   PB[x1t_bank(b, h)][:, :].rearrange("p (k t) -> p k t", k=4), ACT.Copy)\
                       .then_inc(s["x1tsb"], 1)
            for b in range(TB):
                act.wait_ge(s["ract"], b + 1)
                act.activation(lg[:, b, :], lg[:, b, :], ACT.Exp).then_inc(s["rsum"], 1)
            act.wait_ge(s["ysz"], 1)
            act.dma_start(ysb[0:N_EXPERTS, :, :], b_dn[0].rearrange("e (h d) -> e h d", h=2)).then_inc(s["bdn_ld"], 16)
            act.wait_ge(s["wt_ps"], 1)
            act.wait_ge(s["ysz"], 2)
            act.activation(CT[0:N_EXPERTS, :, :].rearrange("p b t -> p (b t)"), PB[4][0:N_EXPERTS, 0:256],
                           ACT.Copy).then_inc(s["ysb_ok"], 1)

            def slots_to_sbuf(h, n):
                act.wait_ge(s["ga"], n)
                act.activation(xg[:, 4 * h:4 * h + 4, :].rearrange("p k s -> p (k s)"), PB[6 + h][:, :], ACT.Copy)\
                   .then_inc(s["xg_ok"], 1)

            slots_to_sbuf(0, 1)
            slots_to_sbuf(1, 2)
            xcount = act.alloc_register("act_extra_blocks")
            act.reg_mov(xcount, 0)

            def extra_slots():
                act.reg_add(xcount, xcount, 1)
                xc = act.snap(xcount, min_val=1, max_val=96)
                act.wait_ge(s["xga"], xc)
                act.activation(yx[:, 0:KT * XSLOTS], PB[6][:, 0:KT * XSLOTS], ACT.Copy).then_inc(s["xxg"], 1)

            def extra_sigmoid():
                act.wait_ge(s["xgok"], act.snap(xcount, min_val=1, max_val=96))
                act.activation(act_x[0:64, :], gt[0:64, :], ACT.Sigmoid, scale=SWIGLU_ALPHA).then_inc(s["xsig"], 1)

            def extra_act_copy():
                xc = act.snap(xcount, min_val=1, max_val=96)
                act.wait_ge(s["xct"], xc)
                act.activation(CTx[:, :, :].rearrange("p b t -> p (b t)"), PB[7][:, 0:256], ACT.Copy)\
                   .then_inc(s["xctd"], 1)
                act.wait_ge(s["xat"], xc)
                act.activation(actTx[:, :, :].rearrange("p c s -> p (c s)"), PB[6][:, 0:256], ACT.Copy)\
                   .then_inc(s["xactT"], 1)

            def extra_outputs():
                act.wait_ge(s["xdnc"], act.snap(act.snap(xcount, min_val=0, max_val=96) * 4 + DN_CHUNKS, min_val=1, max_val=4 * 97))
                act.activation(yx, PB[6][:, :], ACT.Copy).then_inc(s["xyd"], 1)

            with act.Fori(0, PAIRS) as i:
                for e in range(2):
                    E1 = 2 * i + (e + 1)
                    n = act.value_load(nx[0:1, bass.ds(2 * i + e, 1)], min_val=0, max_val=MAX_EXTRA)
                    with act.If(n > 0):
                        extra_slots()
                    act.nop()
                    act.wait_ge(s["g_ok"], E1)
                    act.activation(act_sb, gt, ACT.Sigmoid, scale=SWIGLU_ALPHA).then_inc(s["sig"], 1)
                    with act.If(n > 0):
                        extra_sigmoid()
                    act.nop()
                    if e == 0:
                        act.wait_ge(s["ct"], i + 1)
                        act.activation(CT[:, :, :].rearrange("p b t -> p (b t)"), PB[6][:, 0:256], ACT.Copy)\
                           .then_inc(s["ct_sb"], 1)
                    else:
                        slots_to_sbuf(0, 2 * i + 3)
                        slots_to_sbuf(1, 2 * i + 4)
                    act.wait_ge(s["at"], E1)
                    act.activation(actT[:, :, :].rearrange("p c s -> p (c s)"), PB[6][:, :], ACT.Copy)\
                       .then_inc(s["actT"], 1)
                    with act.If(n > 0):
                        extra_act_copy()
                    act.nop()
                    act.wait_ge(s["dn_used"], E1 * DN_CHUNKS)
                    if e == 0:
                        act.wait_ge(s["comb"], i + 1)
                    act.activation(ysb[64 * e:64 * e + 64, 0, :], PB[7][0:64, :], ACT.Copy)
                    act.activation(ysb[64 * e:64 * e + 64, 1, :], PB[7][64:128, :], ACT.Copy).then_inc(s["ysb_ok"], 1)
                    with act.If(n > 0):
                        extra_outputs()
                    act.nop()
                    with act.If(n > 1):
                        with act.Fori(1, n):
                            extra_slots()
                            extra_sigmoid()
                            extra_act_copy()
                            extra_outputs()
                    act.nop()

        @block.tensor
        def _(pe):
            mm_, tr = pe.matmul, pe.transpose

            def mm(o, l, r, start, stop):
                return mm_(o, l, r, start=start, stop=stop, skip_group_check=True)

            pe.wait_ge(s["x_in"], 16)
            pe.wait_ge(s["cst"], 1)
            for b4 in range(4):
                for k in (2 * b4, 2 * b4 + 1):
                    for b in range(TB):
                        ins = tr(PB[b4][:, (k % 2) * 256 + P * b:(k % 2) * 256 + P * b + P],
                                 x_sb[:, b, P * k:P * k + P], ident)
                ins.then_inc(s["xt_ps"], 1)
            pe.wait_ge(s["rows_ld"], 16 * 8)
            tr(PB[7][:, 0:N_ROWS], rows[0:N_ROWS, :], ident[0:N_ROWS, 0:N_ROWS]).then_inc(s["rows_ps"], 1)
            pe.wait_ge(s["xt_sb"], 4)

            def project(n):
                name = outputs[n]
                base = name.split(".")[0]
                grp = fdict[base][2] if base in fdict else toks[base][3]
                pe.wait_ge(s_win[grp], 16)
                if n >= 2:
                    need(pe, outputs[n - 2])
                ps = PB[n % 2]
                for k in range(KT):
                    if base in fdict:
                        c = fdict[base][1]
                        if base[0] == "q":
                            for g in range(2):
                                h0 = DH * (4 * g + c)
                                ins = mm(ps[64 * g:64 * g + 64, 0:256], w_in_sb[:, k, h0:h0 + DH], xT[:, k, :],
                                         k == 0, k == KT - 1)
                        else:
                            ins = mm(ps[:, 0:256], w_in_sb[:, k, c:c + P], xT[:, k, :], k == 0, k == KT - 1)
                    else:
                        c, w_, _, _ = toks[base]
                        b = int(name[-1])
                        ins = mm(ps[:, 0:w_], xT[:, k, P * b:P * b + P], w_in_sb[:, k, c:c + w_], k == 0, k == KT - 1)
                ins.then_inc(s["proj"], 1)

            for n in range(8):
                project(n)
            pe.wait_ge(s["kvp_ok"], 3)
            pe.wait_ge(s["w1ld"], 32)
            for j in range(16):
                for kv in range(2):
                    t = kvp[kv][j // 8]
                    c = 36 * (j % 8) + 2 * (j // 8)
                    a = t[:, c:c + 32]
                    ins = mm(PB[4][32 * kv:32 * kv + 32, 0:P], a, w1[kv][:, j, :], j == 0, j == 15)
            ins.then_inc(s["hid"], 1)
            project(8)
            pe.wait_ge(s["hid_dve"], 2)
            tr(PB[5][:, 0:64], hx[0:64, :], ident[0:64, 0:64]).then_inc(s["hidt"], 1)
            project(9)
            pe.wait_ge(s["hidt_sb"], 1)
            pe.wait_ge(s["smalls"], 48)
            mm(PB[6][0:64, 0:32], w2sb[:, 0:DH], hidT[:, 0:32], True, True)
            mm(PB[6][64:128, 0:32], w2sb[:, 0:DH], hidT[:, 0:32], True, True)
            mm(PB[7][:, 0:DH], hidV, w2sb[:, DH:2 * DH], True, True).then_inc(s["kcv"], 1)
            project(10)
            pe.wait_ge(s["kcv_sb"], 1)
            need(pe, "q3")
            for b in range(TB):
                for r in range(4):
                    ins = mm(PB[4][:, 128 * b + 32 * r:128 * b + 32 * r + 32], qn[:, r, P * b:P * b + P], kcz,
                             b == 0 and r == 0, True)
            ins.then_inc(s["csc"], 1)
            project(11)

            def scores(u):
                kind, r = units[u]
                q, kz = {"sel": (qn, kzs), "win": (qn, kzw), "fox": (fq, fkz[:, r] if kind == "fox" else None)}[kind]
                if u >= 1:
                    pe.wait_ge(s["ttr"], u)
                if u == NSA:
                    pe.wait_ge(s["fb_ok"], 1)
                b0, b1 = PB[2], PB[3]
                mm(b0[:, 0:256], q[:, r, 0:P], kz[:, :, 0:P], True, True)
                mm(b1[:, :], q[:, r, P:256], kz[:, :, :], True, True).then_inc(s["sc"], 1)

            def transposes(u):
                pe.wait_ge(s["scaled"], u + 1)
                l = L[u % 3]
                for h in range(2):
                    if u >= 1:
                        pe.wait_ge(s["pta" if h == 0 else "ptb"], u)
                    elif h == 0:
                        pe.wait_ge(s["pct_sb"], 1)
                    tr(PB[4 + h][:, 0:P], l[:, P * h:P * h + P], ident)
                    tr(PB[4 + h][:, P:256], l[:, 256 + 256 * h:384 + 256 * h], ident)
                    tr(PB[4 + h][:, 256:384], l[:, 384 + 256 * h:512 + 256 * h], ident).then_inc(s["pts"], 1)

            def values(u):
                kind, r = units[u]
                i = o_index[("nsa", r)] if kind != "fox" else o_index[(kind, r)]
                ps = PB[6 + i % 2]
                if kind != "win" and i >= 2:
                    pe.wait_ge(s["oscaled"], i - 1)
                pe.wait_ge(s["pta"], u + 1)
                pe.wait_ge(s["ptb"], u + 1)
                for h in range(2):
                    c = {"sel": V_SEL + DH * h, "win": V_WIN + DH * h, "fox": V_FOX + P * r + DH * h}[kind]
                    o = ps[64 * h:64 * h + 64, :]
                    p = PT[u % 2][:, 384 * h:384 * h + 384]
                    mm(o[:, 0:256], V[:, 0, c:c + DH], p[:, 0:256], kind != "win", False)
                    ins = mm(o[:, P:256], V[:, 1, c:c + DH], p[:, 256:384], False, kind == "fox")
                    if kind == "win":
                        ins = mm(o[:, 0:256], VCZ[:, 2 * r + h, :], PcT, False, True)
                ins.then_inc(s["pv"], 1)

            for t in range(NSA + 3):
                if t < NSA:
                    scores(t)
                if t == 0:
                    pe.wait_ge(s["pc"], 1)
                    for b in range(TB):
                        ins = tr(PB[5][:, P * b:P * b + P], Lc[:, P * b:P * b + P], ident)
                    ins.then_inc(s["pct"], 1)
                if 2 <= t < NSA + 2:
                    transposes(t - 2)
                if t >= 3:
                    values(t - 3)
                project(len(early) + t)
            project(len(outputs) - 1)
            pe.wait_ge(s["logf"], 1)
            pe.wait_ge(s["tables"], 11)
            pe.wait_ge(s["ttr"], NSA)
            pe.wait_ge(s["ptb"], NSA)
            mm(PB[5][:, 0:4], le_ones[:, 0:P], lf[:, 0, :], True, True)
            mm(PB[5][:, 4:8], le_ones[:, P:256], lf[:, 0, :], False, False)
            mm(PB[5][:, 4:8], le_ones[:, 0:P], lf[:, 1, :], False, True).then_inc(s["clq"], 1)
            pe.wait_ge(s["logf"], 3)
            for h in range(4):
                ps = PB[2 + h // 2][:, 256 * (h % 2):256 * (h % 2) + 256]
                mm(ps, lfb[:, 0, h, :], le_ones, h % 2 == 0, False)
                ins = mm(ps[:, P:256], lfb[:, 1, h, :], le_ones[:, 0:P], False, True)
            ins.then_inc(s["fb_ps"], 1)

            def sb_scores(j):
                mm(PB[0][:, 0:256], bk[:, j, P:256], bqz[:, j, :, P:256], True, True)
                mm(PB[1][:, :], bk[:, j, 0:P], bqz[:, j, :, :], True, True).then_inc(s["zs"], 1)

            def sb_sums(j):
                pe.wait_ge(s["spm"], j + 1)
                v0 = PB[2 * j + 1][:, :].rearrange("p (h t) -> p h t", h=2)
                mm(PB[2 * j + 1][:, :], neg_ge, sp[j][:, 0:512], True, False)
                mm(v0[:, :, P:256], le_ones[:, P:256], sp[j][:, 512:768], False, True)
                mm(PB[2 * j][:, 0:256], neg_ge, sp[j][:, 512:768], True, True).then_inc(s["incl"], 1)

            def sb_values(j):
                i = 6 + j
                pe.wait_ge(s["oscaled"], i - 1)
                pe.wait_ge(s["aexp"], j + 1)
                for h in range(2):
                    c = V_SB + P * j + DH * h
                    o = PB[6 + i % 2][64 * h:64 * h + 64, :]
                    mm(o[:, 0:256], V[:, 0, c:c + DH], zm[j][:, 256 * h:256 * h + 256], True, False)
                    ins = mm(o[:, P:256], V[:, 1, c:c + DH], zm[j][:, 512 + P * h:512 + P * h + P], False, True)
                ins.then_inc(s["pv"], 1)

            def group_squares(g):
                pe.wait_ge(s["ssq_acc"], (3, 4, 5)[g])
                if g > 0:
                    pe.wait_ge(s["rms_in"], g)
                for b in range(TB):
                    mm(PB[0][:, 2 * g + b:2 * g + b + 1], ssq[:, g, P * b:P * b + P], ones1, g == 0 and b == 0,
                       True).then_inc(s["ssqm"], 1)

            def out_project(n):
                g, b, h = op_order[n]
                bank = PB[op_bank[n]]
                pe.wait_ge(s["oscaled"], (4, 6, 8)[g])
                if n >= 5:
                    pe.wait_ge(s["ymix"], n - 4)
                if n == 3:
                    pe.wait_ge(s["pta"], NU)
                if n == 4:
                    pe.wait_ge(s["ptb"], NU)
                for k in op_k[g]:
                    ins = mm(bank[:, :], oT[:, k, P * b:P * b + P], wo_sb[:, k, 512 * h:512 * h + 512],
                             k == op_k[g][0], k == op_k[g][-1])
                ins.then_inc(s["op"], 1)

            for o in outputs[-2:]:
                need(pe, o)
            need(pe, "bk1")
            need(pe, "bq1")
            sb_scores(0)
            scores(NSA)
            pe.wait_ge(s["zcp"], 1)
            sb_scores(1)
            scores(NSA + 1)
            transposes(NSA)
            pe.wait_ge(s["zcp"], 2)
            sb_sums(0)
            pe.wait_ge(s["ttr"], NU)
            sb_sums(1)
            values(NSA)
            transposes(NSA + 1)
            pe.wait_ge(s["wo_ld"], 48)
            pe.wait_ge(s["arg"], 1)
            group_squares(0)
            out_project(0)
            values(NSA + 1)
            pe.wait_ge(s["arg"], 2)
            out_project(1)
            sb_values(0)
            out_project(2)
            sb_values(1)
            out_project(3)
            group_squares(1)
            out_project(4)
            out_project(5)
            group_squares(2)
            for n in range(6, 12):
                out_project(n)
            pe.wait_ge(s["ln_ld"], 48)
            for b in range(TB):
                pe.wait_ge(s["x1ok"], b + 1)
                if b == 1:
                    pe.wait_ge(s["ymix"], 12)
                for h in range(2):
                    for k in range(4):
                        ins = tr(PB[x1t_bank(b, h)][:, P * k:P * k + P], x_sb[:, b, P * (4 * h + k):P * (4 * h + k) + P], ident)
                    ins.then_inc(s["x1t"], 1)
            for b in range(TB):
                pe.wait_ge(s["x1tsb"], 2 * b + 2)
                for k in range(KT):
                    ins = mm(PB[b][:, 0:N_EXPERTS], x1T[:, k, P * b:P * b + P], rw[:, k, :], k == 0, k == KT - 1)
                ins.then_inc(s["lgt"], 1)
            pe.wait_ge(s["route"], 2)
            mm(PB[2][:, 0:32], before[:, 0:P], msk[:, 0, :], True, False)
            mm(PB[2][:, 32:64], before[:, P:256], msk[:, 0, :], False, False)
            mm(PB[2][:, 32:64], before[:, 0:P], msk[:, 1, :], False, False)
            mm(PB[2][:, 64:96], before[:, P:256], msk[:, 0, :], False, False)
            mm(PB[2][:, 64:96], before[:, P:256], msk[:, 1, :], False, True).then_inc(s["cntp"], 1)
            pe.wait_ge(s["routed"], 2)
            for b in range(TB):
                ins = tr(PB[4][0:N_EXPERTS, P * b:P * b + P], lg[:, b, :], ident)
            ins.then_inc(s["wt_ps"], 1)
            acc = lambda b, h: PB[2 * b + h]

            def gather(h):
                for k in range(4):
                    for b in range(TB):
                        ins = mm(PB[6 + h][:, P * k:P * k + P], x_sb[:, b, P * (4 * h + k):P * (4 * h + k) + P],
                                 oh[:, b, :], k == 0 and b == 0, b == TB - 1)
                ins.then_inc(s["ga"], 1)

            def combine():
                for b in range(TB):
                    for h in range(2):
                        ins = mm(acc(b, h)[:, :], CT[:, b, :], ysb[:, h, :], False, False)
                ins.then_inc(s["comb"], 1)

            def gate_up_chunk(c, e):
                for k in range(2 * c, 2 * c + 2):
                    for n in range(4):
                        ins = mm(PB[4 + n // 2][64 * (n % 2):64 * (n % 2) + 64, :], xg[:, k, 64 * e:64 * e + 64],
                                 gu_slot[e][:, k, 512 * n:512 * n + 512], k == 0, False)
                return ins

            def extra_gate_up_chunk(c, e):
                for k in range(2 * c, 2 * c + 2):
                    for n in range(4):
                        ins = mm(PB[6][32 * n:32 * n + 32, :], xgx[:, k, :],
                                 gu_slot[e][:, k, 512 * n:512 * n + 512], k == 0, False)
                return ins

            def gate_up_bias(e):
                for n in range(4):
                    ins = mm(PB[4 + n // 2][64 * (n % 2):64 * (n % 2) + 64, :], sel[:, e, :],
                             bgu[:, 512 * n:512 * n + 512], False, True)
                return ins

            def extra_gate_up_bias(e):
                for n in range(4):
                    ins = mm(PB[6][32 * n:32 * n + 32, :], sel[:, e, 0:XSLOTS], bgu[:, 512 * n:512 * n + 512], False,
                             True)
                return ins

            def gate_up(e, i, extra):
                for c in range(GU_CHUNKS):
                    pe.wait_ge(s_gul[e][c], 16 * i + 16)
                    gate_up_chunk(c, e).then_inc(s["guc"], 1)
                    if extra:
                        extra_gate_up_chunk(c, e).then_inc(s["xguc"], 1)
                if e == 0:
                    pe.wait_ge(s["oht"], i + 1)
                    pe.wait_ge(s["bgu_ld"], 16)
                gate_up_bias(e).then_inc(s["gu"], 1)
                if extra:
                    extra_gate_up_bias(e).then_inc(s["xgu"], 1)

            def down_chunk(c):
                for k in range(2 * c, 2 * c + 2):
                    for h in range(2):
                        ins = mm(PB[7][64 * h:64 * h + 64, :], actT[:, k % 4, 64 * (k // 4):64 * (k // 4) + 64],
                                 dn_slot[:, k, 512 * h:512 * h + 512], k == 0, k == KT - 1)
                return ins

            def extra_down_chunk(c):
                for k in range(2 * c, 2 * c + 2):
                    for h in range(2):
                        r = 64 * h + 32 * (k % 2)
                        ins = mm(PB[6][r:r + 32, :], actTx[:, k % 4, 32 * (k // 4):32 * (k // 4) + 32],
                                 dn_slot[:, k, 512 * h:512 * h + 512], k < 2, k >= KT - 2)
                return ins

            def down(e, i, extra):
                if extra:
                    xc = pe.snap(xcount, min_val=1, max_val=96)
                    pe.wait_ge(s["xctd"], xc)
                    pe.wait_ge(s["xactT"], xc)
                for c in range(DN_CHUNKS):
                    pe.wait_ge(s_dnl[e][c], 16 * i + 16)
                    down_chunk(c).then_inc(s["dn_used"], 1)
                    if extra:
                        extra_down_chunk(c).then_inc(s["xdnc"], 1)

            def act_transposes():
                for c in range(4):
                    ins = tr(PB[6][:, P * c:P * c + P], act_sb[:, P * c:P * c + P], ident)
                return ins

            pe.wait_ge(s["ohs"], 1)
            gather(0)
            gather(1)
            pe.wait_ge(s["ysz"], 1)
            zeros = CTx[:, 0, :].bitcast(BF16)
            for b in range(TB):
                for h in range(2):
                    for q in range(2):
                        mm(acc(b, h)[:, 256 * q:256 * q + 256], zeros[:, 0:P], zeros[:, 0:256], q == 0, False)\
                            .then_inc(s[("xguc", "xdnc")[q]], 1)
            xcount = pe.alloc_register("pe_extra_blocks")
            pe.reg_mov(xcount, 0)

            def extra_gather(outputs_copied):
                pe.reg_add(xcount, xcount, 1)
                xc = pe.snap(xcount, min_val=1, max_val=96)
                pe.wait_ge(s["ysb_ok"], outputs_copied)
                pe.wait_ge(s["xoh"], xc)
                for k in range(KT):
                    for b in range(TB):
                        ins = mm(PB[6][:, XSLOTS * k:XSLOTS * k + XSLOTS], x_sb[:, b, P * k:P * k + P], ohx[:, b, :],
                                 k == 0 and b == 0, b == TB - 1)
                ins.then_inc(s["xga"], 1)
                pe.wait_ge(s["xxg"], xc)

            def extra_act_transposes():
                xc = pe.snap(xcount, min_val=1, max_val=96)
                pe.wait_ge(s["xact"], pe.snap(xc + 1, min_val=2, max_val=97))
                for b in range(TB):
                    ins = tr(PB[7][:, P * b:P * b + P], ohwx[:, b, :], ident)
                ins.then_inc(s["xct"], 1)
                for c in range(4):
                    ins = tr(PB[6][:, 64 * c:64 * c + 64], act_x[0:64, P * c:P * c + P], ident[0:64, 0:64])
                ins.then_inc(s["xat"], 1)

            def extra_combine():
                xc = pe.snap(xcount, min_val=1, max_val=96)
                pe.wait_ge(s["xyd"], xc)
                for b in range(TB):
                    for h in range(2):
                        mm(acc(b, h)[:, :], CTx[64 * h:64 * h + 64, b, :], yx[64 * h:64 * h + 64, :], False, False)

            with pe.Fori(0, PAIRS) as i:
                for e in range(2):
                    E1 = 2 * i + (e + 1)
                    if e == 0:
                        pe.wait_ge(s["xg_ok"], 2 * i + 2)
                    n = pe.value_load(nx[0:1, bass.ds(2 * i + e, 1)], min_val=0, max_val=MAX_EXTRA)
                    with pe.If(n > 0):
                        extra_gather(E1)
                        gate_up(e, i, True)
                    pe.nop()
                    with pe.If(n < 1):
                        gate_up(e, i, False)
                    pe.nop()
                    extra_acts = pe.snap(pe.snap(xcount, min_val=0, max_val=96) + 1, min_val=1, max_val=97)
                    if e == 0:
                        pe.wait_ge(s["ysb_ok"], 2 * i + 1)
                        pe.wait_ge(s["bdn_ld"], 16)
                        combine()
                        pe.wait_ge(s["xact"], extra_acts)
                        tr(PB[6][:, 0:P], ohw[:, 0, :], ident)
                        tr(PB[6][:, P:256], ohw[:, 1, :], ident).then_inc(s["ct"], 1)
                        pe.wait_ge(s["ct_sb"], i + 1)
                    else:
                        pe.wait_ge(s["ohs"], i + 2)
                        pe.wait_ge(s["ysb_ok"], 2 * i + 2)
                        pe.wait_ge(s["xact"], extra_acts)
                        gather(0)
                        gather(1)
                        pe.wait_ge(s["xg_ok"], 2 * i + 4)
                    pe.wait_ge(s["act"], E1)
                    act_transposes().then_inc(s["at"], 1)
                    pe.wait_ge(s["actT"], E1)
                    with pe.If(n > 0):
                        extra_act_transposes()
                    pe.nop()

                    with pe.If(n > 0):
                        down(e, i, True)
                        extra_combine()
                    pe.nop()
                    with pe.If(n < 1):
                        down(e, i, False)
                    pe.nop()
                    with pe.If(n > 1):
                        with pe.Fori(1, n):
                            extra_gather(E1 + 1)
                            for c in range(GU_CHUNKS):
                                extra_gate_up_chunk(c, e).then_inc(s["xguc"], 1)
                            extra_gate_up_bias(e).then_inc(s["xgu"], 1)
                            extra_act_transposes()
                            xc = pe.snap(xcount, min_val=1, max_val=96)
                            pe.wait_ge(s["xctd"], xc)
                            pe.wait_ge(s["xactT"], xc)
                            for c in range(DN_CHUNKS):
                                extra_down_chunk(c).then_inc(s["xdnc"], 1)
                            extra_combine()
                    pe.nop()
            pe.wait_ge(s["ysb_ok"], 2 * PAIRS + 1)
            combine()

        @block.vector
        def _(dve):
            link = chain(dve, "v_self")
            ts, tt, stt, cp = dve.tensor_scalar, dve.tensor_tensor, dve.scalar_tensor_tensor, dve.tensor_copy

            dve.wait_ge(s["tables"], 3)
            for r in range(4):
                for g in range(2):
                    stt(alibi[:, 2 * r + g, :], dist, slope(4 * g + r), causal, ALU.mult, ALU.add)
            for b in (0, 2):
                dve.wait_ge(s["xt_ps"], b + 1)
                cp(xT[:, 2 * b:2 * b + 2, :].rearrange("p k t -> p (k t)"), PB[b][:, :]).then_inc(s["xt_sb"], 1)
            dve.wait_ge(s["rows_ps"], 1)
            cp(cols, PB[7][:, 0:N_ROWS]).then_inc(s["kvp_ok"], 1)
            dve.wait_ge(s["kvp_ok"], 1)
            dve.wait_ge(s["bv_ld"], 64)
            dve.wait_ge(s["zer"], 6)

            def evict(n):
                name = outputs[n]
                if name in by_act:
                    return
                dve.wait_ge(s["proj"], n + 1)
                ps = PB[n % 2]
                base = name.split(".")[0]
                bias = lambda p0, p1: cols[p0:p1, bcol[base]:bcol[base] + 1]
                if base in toks:
                    c, w, at, _ = toks[base]
                    ins = tt(V[:, int(name[-1]), at:at + w], ps[:, 0:w], bV[:, at:at + w], ALU.add)
                elif base[0] == "q":
                    ins = ts(qn[:, int(base[1]), :], ps[:, 0:256], bias(0, P), SCALE, ALU.add, ALU.mult)
                elif base[0] == "f":
                    ins = ts(fq[:, int(base[2]), :], ps[:, 0:256], bias(0, P), SCALE, ALU.add, ALU.mult)
                else:
                    j = int(base[2])
                    ts(bqz[0:64, j, 0, :], ps[0:64, 0:256], bias(0, 64), SCALE, ALU.add, ALU.mult)
                    ins = ts(bqz[64:128, j, 1, :], ps[64:128, 0:256], bias(64, P), SCALE, ALU.add, ALU.mult)
                ins.then_inc(s["ev_dve"], 1)

            dve.wait_ge(s["ev_act"], 2)
            for kv in range(2):
                even = kv2[kv].rearrange("p g (a j e) -> p g a j e", j=8, e=2)[:, :, :, :, 0]
                for v in range(2):
                    c = 16 * kv + 8 * v
                    for g in range(2):
                        ins = tt(kvp[kv][v].rearrange("p (j a g) -> p g a j", j=8, g=2)[:, g], even[:, g],
                                 posT[:, c:c + 8].unsqueeze(1).broadcast_to([P, 18, 8]), ALU.add)
                ins.then_inc(s["kvp_ok"], 1)
            for n in range(8):
                evict(n)
            dve.wait_ge(s["ev_dve"], ready["vw.1"][1])
            ts(gs, V[:, :, V_GATE:V_GATE + 24], -80.0, None, ALU.max).then_inc(s["g_in"], 1)
            dve.wait_ge(s["hid"], 1)
            link(cp(hx[0:64, :], PB[4][0:64, 0:P]))
            link(tt(h2[0:64, :], hx[0:64, :], hx[0:64, :], ALU.mult))
            link(ts(h2[0:64, :], h2[0:64, :], 0.044715 * GELU_C, GELU_C, ALU.mult, ALU.add))
            tt(hu[0:64, :], h2[0:64, :], hx[0:64, :], ALU.mult).then_inc(s["hid_dve"], 1)
            dve.wait_ge(s["hid_act"], 1)
            stt(hx[0:64, :], hu[0:64, :], 1.0, hx[0:64, :], ALU.add, ALU.mult).then_inc(s["hid_dve"], 1)
            evict(8)
            dve.wait_ge(s["masks"], 4)
            for r in range(4):
                for g in range(2):
                    ins = stt(cb[:, :, 2 * r + g, :], dc, slope(4 * g + r), cm, ALU.mult, ALU.add)
            link(ins)
            dve.wait_ge(s["hidt"], 1)
            link(ts(hidT, PB[5][:, 0:64], 0.5, None, ALU.mult))
            for g in range(2):
                ins = cp(hidV.rearrange("p (r g n) -> p r g n", r=4, g=2)[:, :, g, :],
                         hidT[:, 32:64].rearrange("p (n g) -> p g n", g=2)[:, g, :].unsqueeze(1).broadcast_to([P, 4, 16]))
            ins.then_inc(s["hidt_sb"], 1)
            dve.wait_ge(s["g_exp"], 1)
            link(ts(gs, gs, 1.0, None, ALU.add))
            link(dve.reciprocal(gs, gs))
            evict(9)
            dve.wait_ge(s["kcv"], 1)
            kc = PB[6][:, 0:32].rearrange("p (n g) -> p g n", g=2)
            cp(kcz[0:64, 0:16], kc[0:64, 0, :])
            cp(kcz[64:128, 16:32], kc[64:128, 1, :])
            tt(VCZ, PB[7][:, 0:DH].unsqueeze(1).broadcast_to([P, 8, DH]),
               vmask.unsqueeze(2).broadcast_to([P, 8, DH]), ALU.mult).then_inc(s["kcv_sb"], 1)
            evict(10)
            dve.wait_ge(s["csc"], 1)
            link(tt(Lc, PB[4][:, 0:256], cb.rearrange("p b h n -> p (b h n)"), ALU.add))
            Lc3 = Lc.rearrange("p (h n) -> p h n", n=16)
            link(dve.tensor_reduce(cmx, Lc3, AX.X, ALU.max))
            tt(Lc3, Lc3, cmx.unsqueeze(2).broadcast_to([P, 16, 16]), ALU.subtract).then_inc(s["cexp_in"], 1)
            evict(11)

            def compressed_probabilities():
                dve.wait_ge(s["cexp"], 1)
                link(dve.tensor_reduce(csm, Lc3, AX.X, ALU.add))
                link(dve.reciprocal(csm, csm))
                for b in range(TB):
                    c3 = csm[:, 8 * b:8 * b + 8].rearrange("p (r g) -> p r g", g=2)
                    ins = stt(c3, c3, avail[:, b:b + 1], gs[:, b, 0:8].rearrange("p (g r) -> p r g", g=2), ALU.mult,
                              ALU.mult)
                link(ins)
                tt(Lc3, Lc3, csm.unsqueeze(2).broadcast_to([P, 16, 16]), ALU.mult).then_inc(s["pc"], 1)

            def ttr(u):
                kind, r = units[u]
                dve.wait_ge(s["sc"], u + 1)
                if u >= 3:
                    dve.wait_ge(s["pts"], 2 * (u - 2))
                l, m = L[u % 3], mx[u % 3]
                for c in range(4):
                    qb, h = c // 2, c % 2
                    w = (P, 256)[qb]
                    src = PB[2 + qb][:, w * h:w * h + w]
                    tab = (fbias if kind == "fox" else alibi)[:, 2 * r + h, (0, P)[qb]:(P, 384)[qb]]
                    dst = l[:, 256 * qb + w * h:256 * qb + w * h + w]
                    ins = dve.tensor_tensor_reduce(dst, src, tab, 1.0, -3.0e38, ALU.add, ALU.max, m[:, c:c + 1])
                link(ins)
                ts(nmx[u % 3], m, -1.0, None, ALU.mult).then_inc(s["ttr"], 1)

            def scale(u):
                kind, r = units[u]
                dve.wait_ge(s["exp"], u + 1)
                q = rr[u % 3]
                link(dve.reciprocal(q, sm[u % 3]))
                if kind != "fox":
                    n = 8 if kind == "sel" else 16
                    gate = gs[:, :, n:n + 8].rearrange("p b (g r) -> p b g r", g=2)[:, :, :, r]
                    link(tt(q.rearrange("p (b g) -> p b g", b=2), q.rearrange("p (b g) -> p b g", b=2), gate, ALU.mult))
                l = L[u % 3]
                for c, (a, b) in enumerate(((0, 128), (128, 256), (256, 512), (512, 768))):
                    ins = ts(l[:, a:b], l[:, a:b], q[:, c:c + 1], None, ALU.mult)
                ins.then_inc(s["scaled"], 1)

            def ptb(u):
                dve.wait_ge(s["pts"], 2 * u + 2)
                if u >= 2:
                    dve.wait_ge(s["pv"], u - 1)
                cp(PT[u % 2][:, 384:768], PB[5][:, 0:384]).then_inc(s["ptb"], 1)

            def add_square(i):
                kind, r = o_order[i]
                if r > 0:
                    dve.wait_ge(s["oscaled"], i + 1)
                    a = ssq[:, {"nsa": 0, "fox": 1, "sb": 2}[kind], :]
                    tt(a, a, sq, ALU.add).then_inc(s["ssq_acc"], 1)
                    dve.wait_ge(s["ssq_acc"], sum(1 for _, q in o_order[:i + 1] if q > 0))

            for t in range(NSA + 3):
                if t < NSA:
                    ttr(t)
                if t == 0:
                    compressed_probabilities()
                if 1 <= t < NSA + 1:
                    scale(t - 1)
                if 2 <= t < NSA + 2:
                    ptb(t - 2)
                if t >= 3 and units[t - 3][0] == "win":
                    add_square(o_index[("nsa", units[t - 3][1])])
                evict(len(early) + t)
                if t == 7:
                    dve.wait_ge(s["lf_act"], 1)
                    stt(lf, V[:, :, V_F:V_F + 4], 0.0, lt, ALU.min, ALU.subtract).then_inc(s["logf"], 1)
            evict(len(outputs) - 1)
            dve.wait_ge(s["logf"], 1)
            dve.wait_ge(s["proj"], len(outputs))
            for b in range(TB):
                cp(lfb[:, b, :, :], lf[:, b, :].unsqueeze(2).broadcast_to([P, 4, P])).then_inc(s["logf"], 1)
            dve.wait_ge(s["clq"], 1)
            link(cp(ncq.rearrange("p b h -> p (b h)"), PB[5][:, 0:8]))
            dve.wait_ge(s["fb_ps"], 1)
            for h in range(4):
                ps = PB[2 + h // 2][:, 256 * (h % 2):256 * (h % 2) + 256]
                stt(fbias[:, h, 0:P], ps[:, 0:P], ncq[:, 0, h:h + 1], causal[:, 0:P], ALU.subtract, ALU.add)
                ins = stt(fbias[:, h, P:384], ps, ncq[:, 1, h:h + 1], causal[:, P:384], ALU.subtract, ALU.add)
            ins.then_inc(s["fb_ok"], 1)
            dve.wait_ge(s["fb_ok"], 1)

            def copy_sb_scores(j):
                dve.wait_ge(s["zs"], j + 1)
                cp(zc[j][:, 512:768], PB[0][:, 0:256])
                cp(zc[j][:, 0:512], PB[1][:, :]).then_inc(s["zcp"], 1)

            def softplus(j):
                dve.wait_ge(s["sps"], j + 1)
                dve.wait_ge(s["zmk"], j + 1)
                link(stt(sp[j], zc[j], 0.0, sp[j], ALU.max, ALU.add))
                tt(sp[j], sp[j], strict_01, ALU.mult).then_inc(s["spm"], 1)

            def sb_exponent(j):
                dve.wait_ge(s["incl"], j + 1)
                tt(zm[j][:, 512:768], zm[j][:, 512:768], PB[2 * j][:, 0:256], ALU.add)
                tt(zm[j][:, 0:512], zm[j][:, 0:512], PB[2 * j + 1][:, :], ALU.add).then_inc(s["arg"], 1)

            copy_sb_scores(0)
            ttr(NSA)
            copy_sb_scores(1)
            scale(NSA)
            ttr(NSA + 1)
            softplus(0)
            softplus(1)
            scale(NSA + 1)
            ptb(NSA)
            sb_exponent(0)
            sb_exponent(1)
            ptb(NSA + 1)

            def mean_square(g):
                dve.wait_ge(s["ssqm"], 2 * g + 2)
                ts(rms[:, 2 * g:2 * g + 2], PB[0][:, 2 * g:2 * g + 2], 1.0 / (512, 256, 256)[g], RMS_EPS, ALU.mult,
                   ALU.add).then_inc(s["rms_in"], 1)

            def add_mixed(n):
                g, b, h = op_order[n]
                dve.wait_ge(s["op"], n + 1)
                dve.wait_ge(s["rms_p"], g + 1)
                if n > 0:
                    dve.wait_ge(s["ymix"], n)
                yh = y[:, b, 512 * h:512 * h + 512]
                stt(yh, PB[op_bank[n]][:, :], rms[:, 2 * g + b:2 * g + b + 1], yh, ALU.mult, ALU.add)\
                    .then_inc(s["ymix"], 1)

            mean_square(0)
            dve.wait_ge(s["xa"], 1)
            add_mixed(0)
            add_square(5)
            add_mixed(1)
            add_mixed(2)
            add_square(7)
            add_mixed(3)
            mean_square(1)
            add_mixed(4)
            add_mixed(5)
            mean_square(2)

            def norm(v, src, b, stats, powered, n, g, bt, dst, last, loaded):
                dve.bn_stats(st[:, 12 * b:12 * b + 6], v[:, b, 0:512])
                link(dve.bn_stats(st[:, 12 * b + 6:12 * b + 12], v[:, b, 512:1024]))
                o = 24 + 4 * b
                link(dve.bn_aggr(st[:, o:o + 2], st[:, 12 * b:12 * b + 12]))
                ts(st[:, o + 1:o + 2], st[:, o + 1:o + 2], LN_EPS, None, ALU.add).then_inc(s[stats], 1)
                dve.wait_ge(s[loaded], n)
                link(stt(v[:, b, :], v[:, b, :], st[:, o:o + 1], g, ALU.subtract, ALU.mult))
                dve.wait_ge(s[powered], b + 1)
                stt(dst[:, b, :], v[:, b, :], st[:, o + 2:o + 3], bt, ALU.mult, ALU.add).then_inc(s[last], 1)

            for b in range(TB):
                for n in ((6, 7), (8, 9, 10, 11))[b]:
                    add_mixed(n)
                dve.wait_ge(s["ymix"], (8, 12)[b])
                norm(y, None, b, "lnstat", "lnp", 48, lng, lnb, x_sb, "x1ok", "ln_ld")
            dve.wait_ge(s["x1ok"], 2)
            dve.memset(CTx, 0.0)
            dve.memset(ysb, 0.0).then_inc(s["ysz"], 1)
            dve.memset(posm[:, N_EXPERTS:, :], NOT_ROUTED)
            dve.memset(wts[:, N_EXPERTS:, :], 0.0)
            for b in range(TB):
                dve.wait_ge(s["lgt"], b + 1)
                link(tt(lg[:, b, :], PB[b][:, 0:N_EXPERTS], rb, ALU.add))
                link(dve.max(m8[:, b, :], lg[:, b, :]))
                link(dve.max_index(idx8[:, 8 * b:8 * b + 8], m8[:, b, :], lg[:, b, :]))
                ts(lg[:, b, :], lg[:, b, :], m8[:, b, 0:1], None, ALU.subtract).then_inc(s["ract"], 1)
                link(cp(idx4f[:, 4 * b:4 * b + 4], idx8[:, 8 * b:8 * b + 4]))
                link(tt(oh4[:, b, :, :], iota_s[:, 0:N_EXPERTS].unsqueeze(2).broadcast_to([P, N_EXPERTS, 4]),
                        idx4f[:, 4 * b:4 * b + 4].unsqueeze(1).broadcast_to([P, N_EXPERTS, 4]), ALU.is_equal))
                dve.tensor_reduce(msk[:, b, :], oh4[:, b, :, :], AX.X, ALU.add).then_inc(s["route"], 1)
            dve.wait_ge(s["route"], 2)
            dve.memset(CT, 0.0).then_inc(s["ysz"], 1)
            for b in range(TB):
                dve.wait_ge(s["rsum"], b + 1)
                link(dve.tensor_tensor_reduce(lg[:, b, :], lg[:, b, :], msk[:, b, :], 1.0, 0.0, ALU.mult, ALU.add,
                                              row1[:, b:b + 1]))
                link(dve.reciprocal(row1[:, b:b + 1], row1[:, b:b + 1]))
                link(ts(lg[:, b, :], lg[:, b, :], row1[:, b:b + 1], None, ALU.mult))
                link(cp(wts[:, 0:N_EXPERTS, b], lg[:, b, :]))
            dve.wait_ge(s["cntp"], 1)
            count = PB[2][:, 64:96]
            n_sum = [oh4[:, 0, 8 * j:8 * j + 8, :].rearrange("p e k -> p (e k)") for j in range(2)]
            link(ts(n_sum[0], count, float(SLOTS), None, ALU.is_gt))
            for j in range(1, MAX_EXTRA):
                dst = nx[:, 0:N_EXPERTS] if j == MAX_EXTRA - 1 else n_sum[j % 2]
                link(stt(dst, count, float(SLOTS + XSLOTS * j), n_sum[(j - 1) % 2], ALU.is_gt, ALU.add))
            for b in range(TB):
                pm = posm[:, 0:N_EXPERTS, b]
                link(stt(pm, PB[2][:, 32 * b:32 * b + 32], -NOT_ROUTED, msk[:, b, :], ALU.add, ALU.mult))
                ts(pm, pm, NOT_ROUTED, None, ALU.add).then_inc(s["routed"], 1)
            dve.wait_ge(s["routed"], 2)

            def one_hots(step):
                ins = None
                for e in range(2):
                    for b in range(TB):
                        pc, wc = curp[:, 2 * e + b:2 * e + b + 1], curw[:, 2 * e + b:2 * e + b + 1]
                        ts(oh[:, b, 64 * e:64 * e + 64], iota_s, pc, None, ALU.is_equal)
                        ins = ts(ohw[:, b, 64 * e:64 * e + 64], iota_s, pc, wc, ALU.is_equal, ALU.mult)
                ins.then_inc(s["ohs"], 1)

            def expert_rows():
                for e in range(2):
                    ins = ts(sel[:, e, :], pidx, ecnt[:, e:e + 1], None, ALU.is_equal)
                ins.then_inc(s["oht"], 1)

            cp(curp, posm[:, 0:2, :].rearrange("p e b -> p (e b)")).then_inc(s["xact"], 1)
            cp(curw, wts[:, 0:2, :].rearrange("p e b -> p (e b)"))
            dve.memset(ecnt[:, 0:1], 0.0)
            link(dve.memset(ecnt[:, 1:2], 1.0))
            one_hots(0)
            expert_rows()

            def activations(gate, up, rows, a, g_ok, clip, upg, sig, done, count):
                g, u, a = gt[0:rows, :], ut[0:rows, :], a[0:rows, :]
                ts(g, gate, LIMIT, None, ALU.min).then_inc(s[g_ok], 1)
                ts(u, up, LIMIT, -LIMIT, ALU.min, ALU.max).then_inc(s[clip], 1)
                dve.wait_ge(s[clip], count)
                stt(u, u, 1.0, g, ALU.add, ALU.mult).then_inc(s[upg], 1)
                dve.wait_ge(s[upg], count)
                dve.wait_ge(s[sig], count)
                tt(a, u, a, ALU.mult).then_inc(s[done], 1)

            xcount = dve.alloc_register("dve_extra_blocks")
            dve.reg_mov(xcount, 0)
            xexperts = dve.alloc_register("dve_experts_with_extra_blocks")
            dve.reg_mov(xexperts, 0)

            def extra_one_hots():
                dve.reg_add(xcount, xcount, 1)
                xc = dve.snap(xcount, min_val=1, max_val=96)
                earlier = dve.snap(xc * 4, min_val=4, max_val=4 * 96)
                dve.wait_ge(s["xin"], dve.snap(xexperts, min_val=1, max_val=N_EXPERTS))
                dve.wait_ge(s["xdnc"], earlier)
                ts(curx, curx, -float(XSLOTS), None, ALU.add).then_inc(s["xcur"], 1)
                dve.wait_ge(s["xcur"], xc)
                for b in range(TB):
                    ts(ohx[:, b, :], iota_s[:, 0:XSLOTS], curx[:, b:b + 1], None, ALU.is_equal)
                    for q in range(4):
                        ins = ts(ohwx[:, b, 32 * q:32 * q + 32], iota_s[:, 0:XSLOTS], curx[:, b:b + 1], xw[:, b:b + 1],
                                 ALU.is_equal, ALU.mult)
                ins.then_inc(s["xoh"], 1)

            def extra_activations(E1):
                xc = dve.snap(xcount, min_val=1, max_val=96)
                dve.wait_ge(s["act"], E1)
                dve.wait_ge(s["xact"], xc)
                dve.wait_ge(s["xgu"], xc)
                activations(PB[6][0:64, :], PB[6][64:128, :], 2 * XSLOTS, act_x, "xgok", "xclip", "xupg", "xsig", "xact", xc)

            with dve.Fori(0, PAIRS) as i:
                for e in range(2):
                    E1 = 2 * i + (e + 1)
                    n = dve.value_load(nx[0:1, bass.ds(2 * i + e, 1)], min_val=0, max_val=MAX_EXTRA)
                    with dve.If(n > 0):
                        ts(curx, posm[:, bass.ds(2 * i + e, 1), :].rearrange("p e b -> p (e b)"), -float(SLOTS - XSLOTS),
                           None, ALU.add)
                        cp(xw, wts[:, bass.ds(2 * i + e, 1), :].rearrange("p e b -> p (e b)")).then_inc(s["xin"], 1)
                        dve.reg_add(xexperts, xexperts, 1)
                        extra_one_hots()
                    dve.nop()
                    dve.wait_ge(s["gu"], E1)
                    activations(PB[4][:, :], PB[5][:, :], P, act_sb, "g_ok", "clip", "upg", "sig", "act", E1)
                    with dve.If(n > 0):
                        extra_activations(E1)
                    dve.nop()
                    if e == 0:
                        cp(curp, posm[:, bass.ds(2 * i + 2, 2), :].rearrange("p e b -> p (e b)"))
                        cp(curw, wts[:, bass.ds(2 * i + 2, 2), :].rearrange("p e b -> p (e b)")).then_inc(s["cur"], 1)
                        dve.wait_ge(s["cur"], i + 1)
                        dve.wait_ge(s["ct"], i + 1)
                        dve.wait_ge(s["ga"], 2 * i + 2)
                        one_hots(1)
                    with dve.If(n > 1):
                        with dve.Fori(1, n):
                            extra_one_hots()
                            extra_activations(E1)
                    dve.nop()
                    if e == 1:
                        ts(ecnt, ecnt, 2.0, None, ALU.add).then_inc(s["cse"], 1)
                        dve.wait_ge(s["cse"], i + 1)
                        expert_rows()
            dve.wait_ge(s["comb"], PAIRS + 1)
            for b in range(TB):
                for h in range(2):
                    ins = stt(yf[:, b, 512 * h:512 * h + 512], x_sb[:, b, 512 * h:512 * h + 512], ALPHA,
                              PB[2 * b + h][:, :], ALU.mult, ALU.add)
                link(ins)
                norm(yf, None, b, "fin", "flnp", 32, fg, fb, yf, "fout", "ln2_ld")

    return nc


_INS = ['x', 'w_in', 'b_in', 'cmp_pos_k', 'cmp_pos_v', 'cmp_w1_k', 'cmp_w2_k', 'cmp_w1_v', 'cmp_w2_v', 'g_out', 'w_out',
        'ln1_g', 'ln1_b', 'router_w', 'router_b', 'w_gate_up', 'b_gate_up', 'w_down', 'b_down', 'ln2_g', 'ln2_b']
_OUTS = [((1, 256, 1024), 'float32')]


def kernel(**inputs):
    import numpy as _np
    import concourse.bacc as _bacc
    from concourse import mybir as _mybir
    from concourse.bass_utils import run_bass_kernel_spmd as _run

    nc = _bacc.Bacc("TRN2", target_bir_lowering=False, num_devices=1)
    arrays, args = {}, []
    for name in _INS:
        a = _np.ascontiguousarray(inputs[name])
        arrays[f"in_{name}_dram"] = a
        args.append(nc.dram_tensor(f"in_{name}_dram", a.shape, _mybir.dt.from_np(a.dtype), kind="ExternalInput").ap())
    for i, (shape, dtype) in enumerate(_OUTS):
        dt = _mybir.dt.from_np(_np.dtype(dtype))
        args.append(nc.dram_tensor(f"out_{i}_dram", shape, dt, kind="ExternalOutput").ap())
    hybrid_layer(nc, *args)
    r = _run(nc, [arrays], core_ids=[0])
    return r.results[0]["out_0_dram"]
```
